# Optimizing a Trainium2 kernel written in Bass

```python
import math
import jax, jax.numpy as jnp
from jax import lax
import numpy as np

D_MODEL = 1024
BATCH = 1
SEQ = 512
DEPTH = 1

MEM_LEN = 256
ROPE_THETA = 10000.0
RMS_EPS = 1e-6
Q_BLOCK = 128

MLA_HEADS = 8
MLA_NOPE = 64
MLA_ROPE = 32
MLA_V = 64
MLA_Q_RANK = 256
MLA_KV_RANK = 128

SWA_HEADS = 8
SWA_KV_HEADS = 2
SWA_HEAD_DIM = 64
SWA_WINDOW = 128

XA_HEADS = 4
XA_HEAD_DIM = 128

N_EXPERTS = 32
TOP_K = 4
D_EXPERT = 1024
SWIGLU_ALPHA = 1.702
SWIGLU_LIMIT = 7.0
MOE_BLOCK = 128

N_BRANCHES = 3

COL_MLA_Q = MLA_Q_RANK
COL_MLA_KV = MLA_KV_RANK
COL_MLA_KR = MLA_ROPE
COL_SWA_Q = SWA_HEADS * SWA_HEAD_DIM
COL_SWA_K = SWA_KV_HEADS * SWA_HEAD_DIM
COL_SWA_V = SWA_KV_HEADS * SWA_HEAD_DIM
COL_XA_Q = XA_HEADS * XA_HEAD_DIM
COL_GATES = N_BRANCHES * D_MODEL
IN_SPLITS = (
    COL_MLA_Q,
    COL_MLA_Q + COL_MLA_KV,
    COL_MLA_Q + COL_MLA_KV + COL_MLA_KR,
    COL_MLA_Q + COL_MLA_KV + COL_MLA_KR + COL_SWA_Q,
    COL_MLA_Q + COL_MLA_KV + COL_MLA_KR + COL_SWA_Q + COL_SWA_K,
    COL_MLA_Q + COL_MLA_KV + COL_MLA_KR + COL_SWA_Q + COL_SWA_K + COL_SWA_V,
    COL_MLA_Q + COL_MLA_KV + COL_MLA_KR + COL_SWA_Q + COL_SWA_K + COL_SWA_V + COL_XA_Q,
)
D_IN_PROJ = COL_MLA_Q + COL_MLA_KV + COL_MLA_KR + COL_SWA_Q + COL_SWA_K + COL_SWA_V + COL_XA_Q + COL_GATES

kernel_name = "hybrid_mla_swa_xattn_moe_layer"

def rms_norm(x, g):
    xf = x.astype(jnp.float32)
    y = xf * lax.rsqrt(jnp.mean(xf * xf, axis=-1, keepdims=True) + RMS_EPS)
    return (y * g.astype(jnp.float32)).astype(x.dtype)

def rope(x, positions):
    d = x.shape[-1]
    inv_freq = ROPE_THETA ** (-jnp.arange(0, d, 2, dtype=jnp.float32) / d)
    ang = positions.astype(jnp.float32)[..., None] * inv_freq
    cos = jnp.cos(ang)[:, :, None, :]
    sin = jnp.sin(ang)[:, :, None, :]
    xf = x.astype(jnp.float32)
    x1, x2 = xf[..., : d // 2], xf[..., d // 2:]
    out = jnp.concatenate([x1 * cos - x2 * sin, x2 * cos + x1 * sin], axis=-1)
    return out.astype(x.dtype)

def mla_attention(q, k, v):
    b, s, h, dq = q.shape
    dv = v.shape[-1]
    nb = s // Q_BLOCK
    scale = 1.0 / math.sqrt(dq)
    qb = q.reshape(b, nb, Q_BLOCK, h, dq).transpose(1, 0, 2, 3, 4)
    kpos = jnp.arange(s)

    def block(args):
        q_blk, start = args
        sc = jnp.einsum('bqhd,bkhd->bhqk', q_blk, k).astype(jnp.float32) * scale
        qpos = start + jnp.arange(Q_BLOCK)
        sc = jnp.where(kpos[None, :] <= qpos[:, None], sc, -jnp.inf)
        p = jax.nn.softmax(sc, axis=-1).astype(v.dtype)
        return jnp.einsum('bhqk,bkhd->bqhd', p, v)

    o = lax.map(block, (qb, jnp.arange(nb) * Q_BLOCK))
    return o.transpose(1, 0, 2, 3, 4).reshape(b, s, h * dv)

def swa_attention(q, k, v, sinks):
    b, s, hq, dh = q.shape
    hkv = k.shape[2]
    grp = hq // hkv
    w = SWA_WINDOW
    nb = s // w
    scale = 1.0 / math.sqrt(dh)
    qb = q.reshape(b, nb, w, hkv, grp, dh)
    kb = k.reshape(b, nb, w, hkv, dh)
    vb = v.reshape(b, nb, w, hkv, dh)
    zpad = jnp.zeros_like(kb[:, :1])
    kk = jnp.concatenate([jnp.concatenate([zpad, kb[:, :-1]], axis=1), kb], axis=2)
    vv = jnp.concatenate([jnp.concatenate([zpad, vb[:, :-1]], axis=1), vb], axis=2)
    sc = jnp.einsum('bnqhgd,bnkhd->bnhgqk', qb, kk).astype(jnp.float32) * scale
    qi = jnp.arange(w)[:, None]
    kj = jnp.arange(2 * w)[None, :]
    diff = qi + w - kj
    band = (diff >= 0) & (diff < w)
    blk_ok = (jnp.arange(nb)[:, None, None] > 0) | (kj >= w)[None]
    mask = band[None] & blk_ok
    sc = jnp.where(mask[None, :, None, None], sc, -jnp.inf)
    sink = jnp.broadcast_to(sinks.astype(jnp.float32).reshape(1, 1, hkv, grp, 1, 1),
                            sc.shape[:-1] + (1,))
    p = jax.nn.softmax(jnp.concatenate([sc, sink], axis=-1), axis=-1)[..., :-1]
    o = jnp.einsum('bnhgqk,bnkhd->bnqhgd', p.astype(v.dtype), vv)
    return o.reshape(b, s, hq * dh)

def cross_attention(q, km, vm):
    scale = 1.0 / math.sqrt(q.shape[-1])
    sc = jnp.einsum('bshd,bmhd->bhsm', q, km).astype(jnp.float32) * scale
    p = jax.nn.softmax(sc, axis=-1).astype(vm.dtype)
    o = jnp.einsum('bhsm,bmhd->bshd', p, vm)
    return o.reshape(q.shape[0], q.shape[1], -1)

def moe_ffn(xt, w_router, b_router, w_gate_up, b_gate_up, w_down, b_down):
    t, d = xt.shape
    tk = t * TOP_K
    logits = (xt @ w_router + b_router).astype(jnp.float32)
    top_vals, top_idx = lax.top_k(logits, TOP_K)
    gates = jax.nn.softmax(top_vals, axis=-1).astype(xt.dtype)
    flat_e = top_idx.reshape(-1)
    order = jnp.argsort(flat_e)
    sorted_e = flat_e[order]
    counts = jax.ops.segment_sum(jnp.ones((tk,), jnp.int32), flat_e, num_segments=N_EXPERTS)
    padded = ((counts + MOE_BLOCK - 1) // MOE_BLOCK) * MOE_BLOCK
    padded_end = jnp.cumsum(padded)
    padded_start = padded_end - padded
    group_start = jnp.cumsum(counts) - counts
    rank = jnp.arange(tk) - group_start[sorted_e]
    dest = padded_start[sorted_e] + rank
    n_blocks = -(-tk // MOE_BLOCK) + N_EXPERTS
    n_rows = n_blocks * MOE_BLOCK
    token_of_row = jnp.full((n_rows,), t, jnp.int32).at[dest].set((order // TOP_K).astype(jnp.int32))
    weight_of_row = jnp.zeros((n_rows,), xt.dtype).at[dest].set(gates.reshape(-1)[order])
    block_expert = jnp.clip(jnp.searchsorted(padded_end, jnp.arange(n_blocks) * MOE_BLOCK, side='right'),
                            0, N_EXPERTS - 1)
    xpad = jnp.concatenate([xt, jnp.zeros((1, d), xt.dtype)], axis=0)

    def expert_block(args):
        rows, e = args
        xb = xpad[rows]
        gu = xb @ w_gate_up[e] + b_gate_up[e]
        x_glu = jnp.minimum(gu[:, :D_EXPERT], SWIGLU_LIMIT)
        x_lin = jnp.clip(gu[:, D_EXPERT:], -SWIGLU_LIMIT, SWIGLU_LIMIT)
        hdn = x_glu * jax.nn.sigmoid(SWIGLU_ALPHA * x_glu) * (x_lin + 1.0)
        return hdn @ w_down[e] + b_down[e]

    y = lax.map(expert_block, (token_of_row.reshape(n_blocks, MOE_BLOCK), block_expert))
    y = y.reshape(n_rows, d) * weight_of_row[:, None]
    out = jnp.zeros((t + 1, d), xt.dtype).at[token_of_row].add(y)
    return out[:t]

def setup_inputs(seed: int = 0) -> dict:
    key = jax.random.key(seed)
    ks = jax.random.split(key, 32)
    f32 = jnp.float32

    def w(k, shape, fan_in):
        return jax.random.normal(k, shape, f32) * (fan_in ** -0.5)

    def gain(k, shape):
        return 1.0 + 0.05 * jax.random.normal(k, shape, f32)

    def bias(k, shape):
        return 0.01 * jax.random.normal(k, shape, f32)

    L = DEPTH
    return {
        "x": jax.random.normal(ks[0], (BATCH, SEQ, D_MODEL), f32),
        "mem": jax.random.normal(ks[1], (BATCH, MEM_LEN, D_MODEL), f32),
        "positions": jnp.broadcast_to(jnp.arange(SEQ, dtype=jnp.int32), (BATCH, SEQ)),
        "g_mix": gain(ks[2], (L, D_MODEL)),
        "w_in": w(ks[3], (L, D_MODEL, D_IN_PROJ), D_MODEL),
        "g_mla_q": gain(ks[4], (L, MLA_Q_RANK)),
        "w_mla_uq": w(ks[5], (L, MLA_Q_RANK, MLA_HEADS * (MLA_NOPE + MLA_ROPE)), MLA_Q_RANK),
        "g_mla_kv": gain(ks[6], (L, MLA_KV_RANK)),
        "w_mla_ukv": w(ks[7], (L, MLA_KV_RANK, MLA_HEADS * (MLA_NOPE + MLA_V)), MLA_KV_RANK),
        "w_mla_o": w(ks[8], (L, MLA_HEADS * MLA_V, D_MODEL), MLA_HEADS * MLA_V),
        "swa_sinks": 0.5 * jax.random.normal(ks[9], (L, SWA_HEADS), f32),
        "w_swa_o": w(ks[10], (L, SWA_HEADS * SWA_HEAD_DIM, D_MODEL), SWA_HEADS * SWA_HEAD_DIM),
        "g_mem": gain(ks[11], (L, D_MODEL)),
        "w_mem_kv": w(ks[12], (L, D_MODEL, 2 * XA_HEADS * XA_HEAD_DIM), D_MODEL),
        "w_xa_o": w(ks[13], (L, XA_HEADS * XA_HEAD_DIM, D_MODEL), XA_HEADS * XA_HEAD_DIM),
        "b_gate": bias(ks[14], (L, COL_GATES)),
        "w_out": w(ks[15], (L, D_MODEL, D_MODEL), D_MODEL),
        "g_ffn": gain(ks[16], (L, D_MODEL)),
        "w_router": w(ks[17], (L, D_MODEL, N_EXPERTS), D_MODEL),
        "b_router": bias(ks[18], (L, N_EXPERTS)),
        "w_gate_up": w(ks[19], (L, N_EXPERTS, D_MODEL, 2 * D_EXPERT), D_MODEL),
        "b_gate_up": bias(ks[20], (L, N_EXPERTS, 2 * D_EXPERT)),
        "w_down": w(ks[21], (L, N_EXPERTS, D_EXPERT, D_MODEL), D_EXPERT),
        "b_down": bias(ks[22], (L, N_EXPERTS, D_MODEL)),
        "g_final": gain(ks[23], (D_MODEL,)),
    }

def reference(x, mem, positions, g_mix, w_in, g_mla_q, w_mla_uq, g_mla_kv, w_mla_ukv, w_mla_o,
              swa_sinks, w_swa_o, g_mem, w_mem_kv, w_xa_o, b_gate, w_out, g_ffn,
              w_router, b_router, w_gate_up, b_gate_up, w_down, b_down, g_final):
    b, s, d = x.shape
    h = x
    for l in range(DEPTH):
        xn = rms_norm(h, g_mix[l])
        proj = xn @ w_in[l]
        cq, ckv, kr, qs, kswa, vswa, qx, gate_logits = jnp.split(proj, IN_SPLITS, axis=-1)

        q_mla = (rms_norm(cq, g_mla_q[l]) @ w_mla_uq[l]).reshape(b, s, MLA_HEADS, MLA_NOPE + MLA_ROPE)
        q_mla = jnp.concatenate([q_mla[..., :MLA_NOPE], rope(q_mla[..., MLA_NOPE:], positions)], axis=-1)
        kv_mla = (rms_norm(ckv, g_mla_kv[l]) @ w_mla_ukv[l]).reshape(b, s, MLA_HEADS, MLA_NOPE + MLA_V)
        k_rope = jnp.broadcast_to(rope(kr[:, :, None, :], positions), (b, s, MLA_HEADS, MLA_ROPE))
        k_mla = jnp.concatenate([kv_mla[..., :MLA_NOPE], k_rope], axis=-1)
        v_mla = kv_mla[..., MLA_NOPE:]
        out_mla = mla_attention(q_mla, k_mla, v_mla) @ w_mla_o[l]

        q_swa = rope(qs.reshape(b, s, SWA_HEADS, SWA_HEAD_DIM), positions)
        k_swa = rope(kswa.reshape(b, s, SWA_KV_HEADS, SWA_HEAD_DIM), positions)
        v_swa = vswa.reshape(b, s, SWA_KV_HEADS, SWA_HEAD_DIM)
        out_swa = swa_attention(q_swa, k_swa, v_swa, swa_sinks[l]) @ w_swa_o[l]

        kv_mem = rms_norm(mem, g_mem[l]) @ w_mem_kv[l]
        m = mem.shape[1]
        k_mem = kv_mem[..., : XA_HEADS * XA_HEAD_DIM].reshape(b, m, XA_HEADS, XA_HEAD_DIM)
        v_mem = kv_mem[..., XA_HEADS * XA_HEAD_DIM:].reshape(b, m, XA_HEADS, XA_HEAD_DIM)
        out_xa = cross_attention(qx.reshape(b, s, XA_HEADS, XA_HEAD_DIM), k_mem, v_mem) @ w_xa_o[l]

        gates = jax.nn.sigmoid((gate_logits + b_gate[l]).astype(jnp.float32)).astype(x.dtype)
        gates = gates.reshape(b, s, N_BRANCHES, d)
        merged = gates[:, :, 0] * out_mla + gates[:, :, 1] * out_swa + gates[:, :, 2] * out_xa
        h = h + merged @ w_out[l]

        hn = rms_norm(h, g_ffn[l]).reshape(b * s, d)
        h = h + moe_ffn(hn, w_router[l], b_router[l], w_gate_up[l], b_gate_up[l],
                        w_down[l], b_down[l]).reshape(b, s, d)
    return rms_norm(h, g_final)


_drawn_inputs = setup_inputs


def setup_inputs(seed=0):
    import zlib

    import numpy as np

    out = dict(_drawn_inputs(seed))
    spreads = {}
    factors = {'swa_sinks': 6.118, 'b_gate': 18.985, 'b_gate_up': 8.0, 'b_down': 8.0, 'g_mla_q': 3.635}
    for name, (base, spread) in spreads.items():
        noise = np.random.default_rng([zlib.crc32(name.encode()), seed]).standard_normal(out[name].shape)
        drawn = base * np.exp(spread * noise) if base else spread * noise
        out[name] = __import__('jax').numpy.asarray(drawn.astype(out[name].dtype))
    for name, factor in factors.items():
        out[name] = (out[name] * factor).astype(out[name].dtype)
    return out
```

```python
from contextlib import ExitStack

import numpy as np
import concourse.bass as bass
from concourse import mybir

P = 128
ALU = mybir.AluOpType
ACT = mybir.ActivationFunctionType
AX = mybir.AxisListType
F32 = mybir.dt.float32
F32R = mybir.dt.float32r
BF16 = mybir.dt.bfloat16
I32 = mybir.dt.int32
U32 = mybir.dt.uint32

D = 1024
SEQ = 512
MEM = 256
T = SEQ // P
M = MEM // P
KT = D // P
EPS = 1e-6
THETA = 10000.0
MLA_H, NOPE, ROPE, VD = 8, 64, 32, 64
QK = NOPE + ROPE
QR, KVR = 256, 128
SWA_H, SWA_KV, SD = 8, 2, 64
GRP = SWA_H // SWA_KV
XA_H, XD = 4, 128
NE, TOPK, DE = 32, 4, 1024
ALPHA, LIMIT = 1.702, 7.0
HALF = DE // 2
CQ, CKV, CKR = 0, QR, QR + KVR
CQS = CKR + ROPE
CKS = CQS + SWA_H * SD
CVS = CKS + SWA_KV * SD
CQX = CVS + SWA_KV * SD
CG = CQX + XA_H * XD
NEG = -1e30
ROUND = 1.5 * 2.0 ** 23
TWO_PI = 2.0 * float(np.pi)
PI_A = 6.28125
PI_B = float(np.float32(TWO_PI - PI_A))
PI_C = float(TWO_PI - PI_A - PI_B)
PI_SAFE = 3.1415925
NOWHERE = float(2 ** 22)
MAX_OVER = 16
CH = 12
RING = 3
RAW = 6


def make_plan():
    panels, chunks, steps = {}, [], []

    def panel(name, weight, col, n, kt, per, outs):
        ids = []
        for k0 in range(0, kt, per):
            ids.append(len(chunks))
            chunks.append((name, weight, col, n, k0, per))
        panels[name] = dict(ids=ids, per=per, n=n, outs=outs)

    def mm(name):
        p = panels[name]
        return [("mm", name, ci, oi) for ci in range(len(p["ids"])) for oi in range(len(p["outs"]))]

    toks = [(t, 0, None) for t in range(T)]
    panel("MK", "w_mem_kv", 0, 512, KT, 4, [(m, 0, 512) for m in range(M)])
    panel("MV", "w_mem_kv", 512, 512, KT, 4, [(m, 0, 512) for m in range(M)])
    panel("P0", "w_in", 0, CQS, KT, 4, [(t, 0, CQS) for t in range(T)])
    panel("UQ", "w_mla_uq", 0, MLA_H * QK, QR // P, 2, [(t, h * 384, 384) for t in range(T) for h in range(2)])
    panel("UKV", "w_mla_ukv", 0, 1024, 1, 1, [(t, h * 512, 512) for t in range(T) for h in range(2)])
    panel("P1", "w_in", CQS, 512, KT, 4, [(t, 0, 512) for t in range(T)])
    panel("P2", "w_in", CKS, 256, KT, 8, [(t, 0, 256) for t in range(T)])
    panel("P3", "w_in", CQX, 512, KT, 4, [(t, 0, 512) for t in range(T)])
    outw = ["w_mla_o", "w_swa_o", "w_xa_o"]
    for b in range(3):
        for hf in range(2):
            panel(f"G{b}{hf}", "w_in", CG + b * D + hf * 512, 512, KT, 4, [(t, 0, 512) for t in range(T)])
            panel(f"O{b}{hf}", outw[b], hf * 512, 512, 4, 4, [(t, 0, 512) for t in range(T)])
    for hf in range(2):
        panel(f"W{hf}", "w_out", hf * 512, 512, KT, 4, [(t, 0, 512) for t in range(T)])

    units = [("mla", h, qt) for h in range(MLA_H) for qt in range(T)]
    units += [("swa", h, n) for h in range(SWA_H) for n in range(T)]
    units += [("xa", h, qt) for h in range(XA_H) for qt in range(T)]

    def attend(first, last, filler):
        n = last - first + 2
        done = 0
        for i in range(n):
            if first + i < last:
                steps.append(("S", first + i))
            if i >= 1 and first + i - 1 < last:
                steps.append(("T", first + i - 1))
            if i >= 2:
                steps.append(("AV", first + i - 2))
            upto = len(filler) * (i + 1) // n
            steps.extend(filler[done:upto])
            done = upto

    steps.append(("norm", 0))
    steps += [("turn", "mem", m, r) for m in range(M) for r in range(2)]
    steps.append(("norm", 1))
    steps += mm("MK")
    steps += [("turn", "x", t, r) for t in range(T) for r in range(2)]
    steps += mm("MV")
    steps += mm("P0")
    steps += [("turn", "kx", j) for j in range(2)]
    steps.append(("norm", 2))
    steps += [("turn", "c", t) for t in range(T)]
    steps += mm("UQ") + mm("UKV")
    steps += [("turn", "qm", h) for h in range(MLA_H)] + [("turn", "km", h) for h in range(MLA_H)]
    fill = mm("P1") + mm("P2") + [("turn", "qs", j) for j in range(GRP)] + mm("P3")
    fill += [("turn", "ks", 0)] + [("turn", "qx", h) for h in range(XA_H)]
    attend(0, 32, fill)
    steps += [("turn", "att", 0, t) for t in range(T)]
    attend(32, 80, mm("G00") + mm("O00") + mm("G01") + mm("O01"))
    for b in (1, 2):
        steps += [("turn", "att", b, t) for t in range(T)]
        steps += mm(f"G{b}0") + mm(f"O{b}0") + mm(f"G{b}1") + mm(f"O{b}1")
    steps += [("turn", "m", t, r) for t in range(T) for r in range(2)]
    steps += mm("W0") + mm("W1")
    return panels, chunks, units, steps


def build_layer(nc, x, mem, positions, g_mix, w_in, g_mla_q, w_mla_uq, g_mla_kv, w_mla_ukv, w_mla_o,
                swa_sinks, w_swa_o, g_mem, w_mem_kv, w_xa_o, b_gate, w_out, g_ffn, w_router, b_router,
                w_gate_up, b_gate_up, w_down, b_down, g_final, out):
    panels, chunks, units, steps = make_plan()
    weights = dict(w_in=w_in, w_mem_kv=w_mem_kv, w_mla_uq=w_mla_uq, w_mla_ukv=w_mla_ukv,
                   w_mla_o=w_mla_o, w_swa_o=w_swa_o, w_xa_o=w_xa_o, w_out=w_out)
    NF = len(chunks)
    U = len(units)

    owner = []
    ticket_of = {}

    def ticket(key, who):
        ticket_of[key] = len(owner)
        owner.append(who)

    for s in steps:
        if s[0] == "turn":
            ticket(s, "v")
        if s[0] == "mm" and s[2] == 0:
            ticket(("out", s[1], s[3]), "a" if s[1][0] == "G" or s[1] in ("UKV",) else "v")
    for t in range(T):
        for r in range(2):
            ticket(("hn", t, r), "a" if r == 0 else "v")
    for name in ("logits", "rank", "count", "ends", "GT"):
        ticket(name, "v")
    for t in range(T):
        for hf in range(2):
            ticket(("bias", t, hf), "v")

    xn_rows = nc.dram_tensor("xn_rows", [SEQ, D], F32, kind="Internal").ap()
    y_rows = nc.dram_tensor("y_rows", [SEQ * TOPK, D], F32, kind="Internal").ap()

    with ExitStack() as ctx:
        base = nc.sbuf_base
        base += (-base) % 64
        K = 1024

        def at(name, shape, dt, kb, extra=0):
            size = int(np.prod(shape[1:])) * (2 if dt == BF16 else 4)
            off = int(kb * K) + extra
            assert base + off + size <= nc.sbuf_top, (name, off, size)
            return nc.alloc_sbuf_tensor_at(name, shape, dt, offset=base + off)

        hi = at("w_hi", [P, RING, 2048], F32R, 0)
        lo = at("w_lo", [P, RING, 2048], F32R, 24)
        raw = at("w_raw", [P, RING, 2048], F32, 48)
        raw_moe = at("w_raw_moe", [P, RAW, 2048], F32, 48)
        xT_hi = at("xT_hi", [P, KT, SEQ], F32R, 72)
        xT_lo = at("xT_lo", [P, KT, SEQ], F32R, 88)
        mT_hi = at("mT_hi", [P, KT, SEQ], F32R, 72)
        mT_lo = at("mT_lo", [P, KT, SEQ], F32R, 88)
        rows = at("rows", [P, M + T, D], F32, 104)
        junkf = at("junkf", [P, D], F32, 148)
        junk = at("junk", [P, D], F32, 128)
        ang = at("ang", [P, T, 48], F32, 132)
        ang_k = at("ang_k", [P, T, 48], F32, 133)
        qT = at("qT", [P, MLA_H, SEQ], F32, 104)
        kT = at("kT", [P, MLA_H, SEQ], F32, 120)
        attT_hi = at("attT_hi", [P, 4, SEQ], F32R, 104)
        attT_lo = at("attT_lo", [P, 4, SEQ], F32R, 112)
        merged = at("merged", [P, T, D], F32, 120)
        hs = at("hs", [P, T, D], F32, 104)
        hnT = at("hnT", [P, KT, SEQ], F32, 120)
        memT_hi = at("memT_hi", [P, KT, MEM], F32R, 136)
        memT_lo = at("memT_lo", [P, KT, MEM], F32R, 144)
        qm = at("qm", [P, T, MLA_H, QK], F32, 136)
        km = at("km", [P, T, MLA_H, QK], F32, 148)
        att_mla = at("att_mla", [P, T, 512], F32, 136)
        gate = at("gate", [P, T, 512], F32, 136)
        probs = at("probs", [P, 2, 512], F32, 144)
        probsT = at("probsT", [P, 2, 512], F32, 148)
        rowsB = at("rowsB", [P, T, 512], F32, 152)
        att_xa = at("att_xa", [P, T, 512], F32, 152)
        gmem_b = at("gmem_b", [P, D], F32, 160)
        gmix_b = at("gmix_b", [P, D], F32, 164)
        cT_hi = at("cT_hi", [P, 3, SEQ], F32R, 160)
        cT_lo = at("cT_lo", [P, 3, SEQ], F32R, 166)
        qsT = at("qsT", [P, GRP, SEQ], F32, 160)
        ksT = at("ksT", [P, SEQ], F32, 168)
        vs = at("vs", [P, T, SWA_KV * SD], F32, 170)
        kmr = at("kmr", [P, M, 512], F32, 172)
        vm = at("vm", [P, T, MLA_H * VD], F32, 172)
        att_swa = at("att_swa", [P, T, 512], F32, 172)
        kxT = at("kxT", [P, XA_H, MEM], F32, 180)
        vx = at("vx", [P, M, 512], F32, 184)
        h = at("h", [P, T, D], F32, 172)
        bg_raw = at("bg_raw", [64, 512], F32, 188)
        cqr = at("cqr", [P, T, QR + KVR], F32, 188)
        gq_b = at("gq_b", [P, QR], F32, 194)
        gkv_b = at("gkv_b", [P, KVR], F32, 195)
        krr = at("krr", [P, T, ROPE], F32, 195.5)
        ks_row = at("ks_row", [P, T, SWA_KV * SD], F32, 188)
        qxT = at("qxT", [P, XA_H, SEQ], F32, 188)
        bb_raw = at("bb_raw", [64, 2 * DE], F32, 188)
        ident = at("ident", [P, P], F32, 196)
        ident_h = at("ident_h", [P, P], BF16, 196.5)
        mask_cur = at("mask_cur", [P, P], BF16, 196.75)
        mask_prev = at("mask_prev", [P, P], BF16, 197)
        zero_h = at("zero_h", [P, P], BF16, 197.25)
        below = at("below", [P, P], F32, 197.5)
        ones = at("ones", [P, P], F32, 198)
        cosv = at("cosv", [P, T, 48], F32, 198.5)
        sinv = at("sinv", [P, T, 48], F32, 199.25)
        sel = at("sel", [64, P], F32R, 200)
        bg = at("bg", [64, 512], F32R, 200.5)
        ropeA = at("ropeA", [P, 512], F32, 202.5)
        ropeB = at("ropeB", [P, 512], F32, 204.5)
        o = int(206.5 * K)
        small = {}
        for name, n in (("nmax", U), ("mx", 8), ("rsum", U), ("esink", 8), ("stat", 32)):
            small[name] = at(name, [P, n], F32, 0, o)
            o += 4 * n
        nmax, mx, rsum, esink, stat = (small[n] for n in ("nmax", "mx", "rsum", "esink", "stat"))
        sink_b = at("sink_b", [P, 8], F32, 0, o)
        nsink_b = at("nsink_b", [P, 8], F32, 0, o + 32)
        rowid = at("rowid", [64, 1], F32, 0, o + 64)
        rowid_i = at("rowid_i", [64, 1], I32, 0, o + 96)
        pos_i = at("pos_i", [P, T], I32, 0, o + 128)
        posf = at("posf", [P, T], F32, 0, o + 160)
        rowid_f = at("rowid_f", [64, 1], F32, 0, o + 224)
        over_n = at("over_n", [1, 1], I32, 0, o + 192)
        inv_f = at("inv_f", [P, 48], F32, 135)
        exT_hi = at("exT_hi", [P, 2, KT, P], F32R, 96)
        exT_lo = at("exT_lo", [P, 2, KT, P], F32R, 104)
        hT_hi = at("hT_hi", [P, KT, P], F32R, 112)
        hT_lo = at("hT_lo", [P, KT, P], F32R, 116)
        g_sb = at("g_sb", [P, 2, HALF], F32, 120)
        u_sb = at("u_sb", [P, 2, HALF], F32, 124)
        s_sb = at("s_sb", [P, 2, HALF], F32, 128)
        h_sb = at("h_sb", [P, 2, HALF], F32, 132)
        xg = at("xg", [P, D], F32, 136)
        y_sb = at("y_sb", [P, D], F32, 140)
        bb = at("bb", [64, 2 * DE], F32R, 144)
        bdn = at("bdn", [NE, D], F32, 152)
        gfin_b = at("gfin_b", [P, D], F32, 156)
        gffn_b = at("gffn_b", [P, D], F32, 160)
        onehot = at("onehot", [P, T, TOPK, NE], F32, 164)
        tmp512 = at("tmp512", [P, T, TOPK, NE], F32, 166)
        picks = at("picks", [P, T, P], F32, 168)
        wr = at("wr", [P, KT, NE], F32, 170)
        lg = at("lg", [P, T, NE], F32, 171)
        br_b = at("br_b", [P, NE], F32, 171.5)
        ecol = at("ecol", [64, NE + MAX_OVER], F32, 171.625)
        slots_f = at("slots_f", [P, P], F32, 198.5)
        rank_e = at("rank_e", [P, T, NE], F32, 199)
        val_e = at("val_e", [P, T, NE], F32, 199.5)
        msk = at("msk", [P, T, NE], F32, 200.5)
        gdense = at("gdense", [P, T, NE], F32, 201)
        over_b = at("over_b", [P, MAX_OVER], F32, 201.5)
        mval = at("mval", [P, T, 8], F32, 201.625)
        midx = at("midx", [P, T, 8], U32, 201.75)
        idxf = at("idxf", [P, T, TOPK], F32, 201.875)
        gk = at("gk", [P, T, TOPK], F32, 201.9375)
        asg_i = at("asg_i", [P, T, TOPK], I32, 202)
        asg_f = at("asg_f", [P, T, TOPK], F32, 202.0625)
        lanes_e = at("lanes_e", [P, NE], F32, 202.125)
        lanes_i = at("lanes_i", [P, P], I32, 202.5)
        over_i = at("over_i", [P, MAX_OVER, NE], F32, 204.5)
        upto32 = at("upto32", [NE, NE], F32, 203)
        over = at("over", [NE, P], F32, 203.125)
        ends = at("ends", [P, NE], F32, 203.625)
        over_e = at("over_e", [P, MAX_OVER], F32, 203.75)
        over_ei = at("over_ei", [P, MAX_OVER], I32, 203.8125)
        rank_o = at("rank_o", [P, T], F32, 203.875)
        asg_sb = at("asg_sb", [P, 2], U32, 203.9375)
        tok_sb = at("tok_sb", [P, 2], U32, 204)
        idx_t = at("idx_t", [P, 2], F32, 204.0625)
        rank_c = at("rank_c", [P, T], F32, 204.125)
        GT = at("GT", [NE, SEQ], F32, 166)
        yk = at("yk", [P, T, TOPK, D], F32, 0)
        fin = at("fin", [P, T, D], F32, 64)
        junk2 = at("junk2", [P, D], F32, 80)

        PA = [ctx.enter_context(nc.psum_tensor(f"PA{i}", [P, 512], F32)) for i in range(4)]
        SC = [ctx.enter_context(nc.psum_tensor(f"SC{i}", [P, 512], F32)) for i in range(2)]
        PTb = ctx.enter_context(nc.psum_tensor("PTb", [P, 512], F32))
        OB = ctx.enter_context(nc.psum_tensor("OB", [P, 512], F32))

        def sem(name):
            return ctx.enter_context(nc.semaphore(name))

        consts = sem("consts")
        rows_in = [sem(f"rows_in{i}") for i in range(M + T)]
        gmem_in, gmix_in, pos_in, bg_in = (sem(n) for n in ("gmem_in", "gmix_in", "pos_in", "bg_in"))
        gq_in, gkv_in = sem("gq_in"), sem("gkv_in")
        raw_in = [sem(f"raw_in{i}") for i in range(RING)]
        moe_in = [sem(f"moe_in{i}") for i in range(RAW)]
        hi_ready, lo_ready, used = sem("hi_ready"), sem("lo_ready"), sem("used")
        ticket_done = sem("ticket_done")
        free_v, free_a = sem("free_v"), sem("free_a")
        part_hi = sem("part_hi")
        sq_done, var_done, root_done = sem("sq_done"), sem("var_done"), sem("root_done")
        normed = sem("normed")
        sel_ready, bg_hi, bg_ready = sem("sel_ready"), sem("bg_hi"), sem("bg_ready")
        trig, trig_ready = sem("trig"), sem("trig_ready")
        row_ready = sem("row_ready")
        row_k = sem("row_k")
        s_done, nm_done, exp_done, es_done = sem("s_done"), sem("nm_done"), sem("exp_done"), sem("es_done")
        t_done, pt_done, av_done, o_done = sem("t_done"), sem("pt_done"), sem("av_done"), sem("o_done")
        h_in, late_in = sem("h_in"), sem("late_in")
        dve_chain = sem("dve_chain")
        hs_ready, hs_stored = sem("hs_ready"), sem("hs_stored")
        mask_ready, over_ready, gd_ready = sem("mask_ready"), sem("over_ready"), sem("gd_ready")
        sub_done, gexp_done = sem("sub_done"), sem("gexp_done")
        bb_hi, bb_ready = sem("bb_hi"), sem("bb_ready")
        route_ready, list_ready, gt_ready = sem("route_ready"), sem("list_ready"), sem("gt_ready")
        xg_clear = sem("xg_clear")
        pick_ready, pick_summed, tok_ready = sem("pick_ready"), sem("pick_summed"), sem("tok_ready")
        shift_ready, rank_copied = sem("shift_ready"), sem("rank_copied")
        xg_in, xt_turned, xt_hi, xt_ready = sem("xg_in"), sem("xt_turned"), sem("xt_hi"), sem("xt_ready")
        gu_done, g_ready, sig_ready, hid_ready = sem("gu_done"), sem("g_ready"), sem("sig_ready"), sem("hid_ready")
        ht_turned, ht_hi, ht_ready = sem("ht_turned"), sem("ht_hi"), sem("ht_ready")
        y_ready, y_stored = sem("y_ready"), sem("y_stored")
        pool_awake = sem("pool_awake")
        yk_in = [sem(f"yk_in{t}") for t in range(T)]
        find_chain, glu_chain = sem("find_chain"), sem("glu_chain")
        h_final, fsq, fvar, froot, fin_ready, out_done = (sem(n) for n in ("h_final", "fsq", "fvar", "froot", "fin_ready", "out_done"))

        NCONST = 12
        LATE = 7

        def unit_size(unit):
            kind, _, qt = unit
            if kind == "mla":
                return (qt + 1) * P, QK ** -0.5
            if kind == "swa":
                return (P if qt == 0 else 2 * P), SD ** -0.5
            return MEM, XD ** -0.5

        def freed(n):
            who = owner[n]
            return (free_v if who == "v" else free_a), sum(1 for w in owner[:n + 1] if w == who)

        def final_chunk(c):
            return c == panels[chunks[c][0]]["ids"][-1]

        def used_up(c):
            if final_chunk(c):
                name = chunks[c][0]
                return ticket_done, ticket_of[("out", name, len(panels[name]["outs"]) - 1)] + 1
            return used, sum(1 for d in range(c + 1) if not final_chunk(d))

        NU = sum(1 for c in range(NF) if not final_chunk(c))

        def take(eng, key):
            n = ticket_of[key]
            if n >= 4:
                eng.wait_ge(*freed(n - 4))
            return PA[n % 4]

        def bank(key):
            return PA[ticket_of[key] % 4]

        block = ctx.enter_context(nc.Block())

        @block.sync
        def _(sp):
            def rows_load(i):
                src = mem[0, i * P:(i + 1) * P, :] if i < M else x[0, (i - M) * P:(i - M + 1) * P, :]
                sp.dma_start(rows[:, i, :], src).then_inc(rows_in[i], 16)

            def chunk_load(c):
                name, w, col, n, k0, per = chunks[c]
                src = weights[w][0, k0 * P:(k0 + per) * P, col:col + n].rearrange("(k p) n -> p k n", p=P)
                dst = raw[:, c % RING, 0:per * n].rearrange("p (k n) -> p k n", k=per)
                if c >= RING:
                    sp.wait_ge(lo_ready, c - RING + 1)
                sp.dma_start(dst, src).then_inc(raw_in[c % RING], 16)

            rows_load(0)
            rows_load(1)
            sp.dma_start(gmem_b[:, :], g_mem[0:1, :].to_broadcast([P, D])).then_inc(gmem_in, 16)
            chunk_load(0)
            for i in range(M, M + T):
                rows_load(i)
            sp.dma_start(gmix_b[:, :], g_mix[0:1, :].to_broadcast([P, D])).then_inc(gmix_in, 16)
            chunk_load(1)
            chunk_load(2)
            sp.dma_start(pos_i[:, :], positions[0].rearrange("(t p) -> p t", p=P), allow_slow_non_contiguous=True).then_inc(pos_in, 16)
            sp.wait_ge(consts, NCONST)
            for part in range(2):
                sp.dma_start(bg_raw[32 * part:32 * part + 6, :],
                             b_gate[0].rearrange("(j n) -> j n", n=512)).then_inc(bg_in, 16)
            sp.dma_start(gq_b[:, :], g_mla_q[0:1, :].to_broadcast([P, QR])).then_inc(gq_in, 16)
            sp.dma_start(gkv_b[:, :], g_mla_kv[0:1, :].to_broadcast([P, KVR])).then_inc(gkv_in, 16)
            for c in range(RING, panels["O21"]["ids"][0] + 1):
                chunk_load(c)
            sp.wait_ge(*used_up(panels["O20"]["ids"][0]))
            sp.dma_start(h[:, :, :], x[0].rearrange("(t p) d -> p t d", p=P)).then_inc(h_in, 16)
            chunk_load(panels["W0"]["ids"][0])
            sp.dma_start(gffn_b[:, :], g_ffn[0:1, :].to_broadcast([P, D])).then_inc(late_in, 16)
            sp.dma_start(wr[:, :, :], w_router[0].rearrange("(k p) e -> p k e", p=P)).then_inc(late_in, 16)
            sp.dma_start(br_b[:, :], b_router[0:1, :].to_broadcast([P, NE])).then_inc(late_in, 16)
            for part in range(2):
                sp.dma_start(bb_raw[32 * part:32 * part + 32, :], b_gate_up[0]).then_inc(late_in, 16)
            sp.dma_start(bdn[:, :], b_down[0]).then_inc(late_in, 16)
            sp.dma_start(gfin_b[:, :], g_final.rearrange("(a d) -> a d", a=1).to_broadcast([P, D])).then_inc(late_in, 16)
            for c in range(panels["W0"]["ids"][0] + 1, NF):
                chunk_load(c)
            sp.wait_ge(*used_up(NF - 1))

            def expert_load(e, cc, n):
                slot = cc % RAW
                sp.wait_ge(lo_ready, n * CH + (NF + cc - RAW + 1))
                dst = raw_moe[:, slot, :]
                if cc < 8:
                    hf, k0 = cc // 4, (cc % 4) * 2
                    for k in range(2):
                        src = w_gate_up[0, bass.ds(e, 1), (k0 + k) * P:(k0 + k + 1) * P, :] \
                            .rearrange("o p (s f n) -> (o p) s f n", s=2, f=2)[:, :, hf, :]
                        sp.dma_start(dst[:, k * 1024:(k + 1) * 1024].rearrange("p (s n) -> p s n", s=2),
                                     src).then_inc(moe_in[slot], 16)
                else:
                    k0 = (cc - 8) * 2
                    src = w_down[0, bass.ds(e, 1), k0 * P:(k0 + 2) * P, :].rearrange("o (k p) n -> (o p) k n", p=P)
                    sp.dma_start(dst.rearrange("p (k n) -> p k n", k=2), src).then_inc(moe_in[slot], 32)

            with sp.Fori(0, NE // 2) as i:
                for par in range(2):
                    for cc in range(CH):
                        expert_load(i * 2 + par, cc, i * 2 + par)
            sp.wait_ge(list_ready, 1)
            n_over = sp.value_load(over_n[0:1, 0:1], min_val=0, max_val=MAX_OVER)
            with sp.Fori(0, MAX_OVER) as j:
                with sp.If(j < n_over):
                    e = sp.value_load(over_ei[0:1, bass.ds(j, 1)], min_val=0, max_val=NE - 1)
                    for cc in range(CH):
                        expert_load(e, cc, j + NE)
            sp.wait_ge(y_stored, n_over * 16 + 16 * (NE + 1))
            for t in range(T):
                sp.dma_start(yk[:, t, :, :], y_rows[t * P * TOPK:(t + 1) * P * TOPK, :]
                             .rearrange("(p k) d -> p k d", k=TOPK)).then_inc(yk_in[t], 16)
            for t in range(T):
                sp.wait_ge(fin_ready, t + 1)
                sp.dma_start(out[0, t * P:(t + 1) * P, :], fin[:, t, :]).then_inc(out_done, 16)
            sp.wait_ge(out_done, 16 * T)

        @block.gpsimd
        def _(pool):
            def done(ins):
                ins.then_inc(consts, 1)

            pool.dma_start(sink_b[:, :], swa_sinks[0:1, :].to_broadcast([P, SWA_H])).then_inc(y_stored, 16)
            pool.sem_inc(y_ready, 2)
            pool.sem_inc(gu_done, 2)
            pool.memset(zero_h[:, :], 0.0).then_inc(consts, 1)
            pool.memset(ident[:, :], 0.0).then_inc(consts, 1)
            pool.memset(below[:, :], 1.0).then_inc(consts, 1)
            pool.memset(bg_raw[:, :], 0.0).then_inc(consts, 1)
            for a, n in ((0, 32), (32, 16)):
                for i in range(n):
                    last = pool.memset(inv_f[:, a + i:a + i + 1], float(np.float32(THETA ** (-i / n))))
            last.then_inc(consts, 1)
            pool.iota(rowid_i[:, :], [[0, 1]], channel_multiplier=1).then_inc(consts, 1)
            pool.memset(ones[:, :], 1.0).then_inc(consts, 1)
            pool.wait_ge(consts, 7)
            done(pool.affine_select(out=ident[:, :], in_=ident[:, :], compare_op=ALU.not_equal, fill=1.0,
                                    base=0, pattern=[[-1, P]], channel_multiplier=1))
            done(pool.affine_select(out=ident_h[:, :], in_=zero_h[:, :], compare_op=ALU.not_equal, fill=1.0,
                                    base=0, pattern=[[-1, P]], channel_multiplier=1))
            done(pool.affine_select(out=mask_cur[:, :], in_=zero_h[:, :], compare_op=ALU.is_ge, fill=NEG,
                                    base=0, pattern=[[-1, P]], channel_multiplier=1))
            done(pool.affine_select(out=mask_prev[:, :], in_=zero_h[:, :], compare_op=ALU.is_gt, fill=NEG,
                                    base=0, pattern=[[1, P]], channel_multiplier=-1))
            done(pool.affine_select(out=below[:, :], in_=below[:, :], compare_op=ALU.is_gt, fill=0.0,
                                    base=0, pattern=[[1, P]], channel_multiplier=-1))

            pool.wait_ge(*used_up(NF - 1))
            pool.wait_ge(free_a, sum(1 for k, n in ticket_of.items() if k[0] != "hn" and owner[n] == "a"))
            pool.iota(lanes_i[:, :], [[1, P]], channel_multiplier=0).then_inc(route_ready, 1)
            pool.iota(asg_i[:, :, :], [[P * TOPK, T], [1, TOPK]], base=1, channel_multiplier=TOPK).then_inc(route_ready, 1)
            pool.iota(over_i[:, :, :], [[1, MAX_OVER], [0, NE]], channel_multiplier=0,
                      allow_small_or_imprecise_dtypes=True).then_inc(route_ready, 1)
            pool.memset(upto32[:, :], 1.0).then_inc(route_ready, 1)
            pool.memset(xg[:, :], 0.0).then_inc(xg_clear, 1)
            pool.wait_ge(route_ready, 4)
            pool.tensor_copy(slots_f[:, :], lanes_i[:, :]).then_inc(route_ready, 1)
            pool.tensor_copy(lanes_e[:, :], lanes_i[:, 0:NE]).then_inc(route_ready, 1)
            pool.tensor_copy(asg_f[:, :, :], asg_i[:, :, :]).then_inc(route_ready, 1)
            pool.tensor_copy(ecol[:, 0:NE], lanes_i[0:64, 0:NE]).then_inc(route_ready, 1)
            pool.affine_select(out=upto32[:, :], in_=upto32[:, :], compare_op=ALU.is_ge, fill=0.0,
                               base=0, pattern=[[1, NE]], channel_multiplier=-1).then_inc(route_ready, 1)
            pool.wait_ge(route_ready, 9)

            def pick(ranks, n):
                pool.wait_ge(pick_summed, n)
                pool.sem_inc(pool_awake, 1)
                for t in range(T):
                    last = pool.tensor_scalar(picks[:, t, :], slots_f[:, :], ranks[:, t:t + 1], None, ALU.is_equal)
                last.then_inc(pick_ready, 1)

            def pick_expert(e, n):
                pool.wait_ge(pick_summed, n)
                pool.tensor_copy(rank_c[:, :], rank_e[:, :, e].rearrange("p t o -> p (t o)")).then_inc(rank_copied, 1)
                pool.wait_ge(rank_copied, n + 1)
                pool.sem_inc(pool_awake, 1)
                pick(rank_c, n)

            def gather(par, n):
                pool.wait_ge(tok_ready, n + 1)
                pool.wait_ge(xt_turned, n * 2)
                pool.sem_inc(pool_awake, 1)
                pool.indirect_dma_start(xg[:, :], None, xn_rows,
                                        bass.IndirectOffsetOnAxis(ap=tok_sb[:, par:par + 1], axis=0),
                                        bounds_check=SEQ - 1, oob_is_err=False).then_inc(xg_in, 16)

            def scatter(par, n):
                pool.wait_ge(y_ready, n * 2 + 4)
                pool.sem_inc(pool_awake, 1)
                pool.indirect_dma_start(y_rows, bass.IndirectOffsetOnAxis(ap=asg_sb[:, par:par + 1], axis=0),
                                        y_sb[:, :], None,
                                        bounds_check=SEQ * TOPK - 1, oob_is_err=False).then_inc(y_stored, 16)

            pool.wait_ge(mask_ready, 2)
            pick_expert(slice(0, 1), 0)
            pool.wait_ge(xg_clear, 1)
            pool.wait_ge(hs_stored, 16 * T)
            gather(0, 0)

            def body(e, par, ahead):
                if ahead:
                    pick_expert(bass.ds(e + 1, 1), e + 1)
                    gather((par + 1) % 2, e + 1)
                scatter(par, e)

            with pool.Fori(0, NE // 2 - 1) as i:
                for par in range(2):
                    body(i * 2 + par, par, True)
            body(NE - 2, 0, True)
            body(NE - 1, 1, False)

            pool.wait_ge(list_ready, 1)
            n_over = pool.value_load(over_n[0:1, 0:1], min_val=0, max_val=MAX_OVER)
            with pool.Fori(0, MAX_OVER) as j:
                with pool.If(j < n_over):
                    pool.wait_ge(shift_ready, j + 1)
                    pick(rank_o, j + NE)
                    pool.wait_ge(y_stored, j * 16 + 16 * (NE + 1))
                    gather(0, j + NE)
                    scatter(0, j + NE)

        @block.scalar
        def _(act):
            def split(c):
                per, n = chunks[c][5], chunks[c][3]
                act.wait_ge(raw_in[c % RING], 16 * (c // RING + 1))
                if c >= RING:
                    act.wait_ge(*used_up(c - RING))
                act.activation(hi[:, c % RING, 0:per * n], raw[:, c % RING, 0:per * n], ACT.Copy).then_inc(hi_ready, 1)

            squares = [0]

            def square(src, col):
                if squares[0]:
                    act.wait_ge(sq_done, squares[0])
                squares[0] += 1
                act.activation(junk[:, 0:src.shape[-1]], src, ACT.Square,
                               accum_out=stat[:, col:col + 1]).then_inc(sq_done, 1)

            act.wait_ge(trig, 1)
            act.activation(sinv[:, :, :], ang[:, :, :], ACT.Sin).then_inc(trig_ready, 1)
            act.wait_ge(trig, 2)
            act.activation(cosv[:, :, :], ang_k[:, :, :], ACT.Sin).then_inc(trig_ready, 1)
            act.wait_ge(bg_in, 32)
            act.activation(bg[:, :], bg_raw[:, :], ACT.Copy).then_inc(bg_hi, 1)
            for c in range(RING):
                split(c)
            roots = 0
            for s in steps:
                if s[0] == "norm":
                    lo_i, hi_i = ((0, M), (M, M + T))[s[1]] if s[1] < 2 else (0, 0)
                    for i in range(lo_i, hi_i):
                        act.wait_ge(rows_in[i], 16)
                        square(rows[:, i, :], i)
                    roots += 1
                    act.wait_ge(var_done, roots)
                    a, b = ((0, M), (M, M + T), (8, 16))[s[1]]
                    act.activation(stat[:, a:b], stat[:, a:b], ACT.Sqrt).then_inc(root_done, 1)
                elif s[0] == "turn":
                    kind, n = s[1], ticket_of[s]
                    pb = bank(s)
                    if kind in ("mem", "x", "c", "att", "m"):
                        act.wait_ge(ticket_done, n + 1)
                        v = pb[:, :].rearrange("p (k n) -> p k n", n=P)
                        sc = 1.0
                        if kind == "mem":
                            dst = memT_hi[:, 4 * s[3]:4 * s[3] + 4, s[2] * P:(s[2] + 1) * P]
                        elif kind == "x":
                            dst = xT_hi[:, 4 * s[3]:4 * s[3] + 4, s[2] * P:(s[2] + 1) * P]
                        elif kind == "c":
                            dst, v = cT_hi[:, :, s[2] * P:(s[2] + 1) * P], v[:, 0:3, :]
                        elif kind == "att":
                            dst = attT_hi[:, :, s[3] * P:(s[3] + 1) * P]
                        else:
                            dst, sc = mT_hi[:, 4 * s[3]:4 * s[3] + 4, s[2] * P:(s[2] + 1) * P], 0.5
                        act.activation(dst, v, ACT.Copy, scale=sc).then_inc(part_hi, 1)
                elif s[0] == "mm":
                    _, name, ci, oi = s
                    p = panels[name]
                    last = ci == len(p["ids"]) - 1
                    key = ("out", name, oi)
                    if last and name == "P0":
                        act.wait_ge(ticket_done, ticket_of[key] + 1)
                        square(bank(key)[:, CQ:CQ + QR], 8 + oi)
                        square(bank(key)[:, CKV:CKV + KVR], 12 + oi)
                    elif last and name == "UKV":
                        t, half = oi // 2, oi % 2
                        act.wait_ge(ticket_done, ticket_of[key] + 1)
                        v = bank(key)[:, :].rearrange("p (h d) -> p h d", h=4)
                        act.activation(km[:, t, 4 * half:4 * half + 4, 0:NOPE], v[:, :, 0:NOPE], ACT.Copy).then_inc(row_k, 1)
                        act.activation(vm[:, t, 256 * half:256 * half + 256].rearrange("p (h d) -> p h d", h=4),
                                       v[:, :, NOPE:NOPE + VD], ACT.Copy).then_inc(free_a, 1)
                    elif last and name[0] == "G":
                        act.wait_ge(ticket_done, ticket_of[key] + 1)
                        b, hf = int(name[1]), int(name[2])
                        if (b, hf) != (0, 0):
                            prev = f"O{b}{hf - 1}" if hf else f"O{b - 1}1"
                            act.wait_ge(*freed(ticket_of[("out", prev, oi)]))
                        act.activation(gate[:, oi, :], bank(key)[:, :], ACT.Tanh, scale=0.5).then_inc(free_a, 1)
                    if oi == len(p["outs"]) - 1 and p["ids"][ci] + RING < NF:
                        split(p["ids"][ci] + RING)
                elif s[0] == "S":
                    u = s[1]
                    kind, hh, _ = units[u]
                    act.wait_ge(nm_done, u + 1)
                    if u >= 2:
                        act.wait_ge(t_done, u - 1)
                    if kind == "swa":
                        if u - 32 >= 8:
                            act.wait_ge(o_done, u - 7)
                        act.activation(esink[:, u % 8:u % 8 + 1], nmax[:, u:u + 1], ACT.Exp,
                                       bias=sink_b[:, hh:hh + 1]).then_inc(es_done, 1)
                    n, scale = unit_size(units[u])
                    act.activation(probs[:, u % 2, 0:n], SC[u % 2][:, 0:n], ACT.Exp, bias=nmax[:, u:u + 1], scale=scale,
                                   accum_out=rsum[:, u:u + 1]).then_inc(exp_done, 1)
                elif s[0] == "T":
                    u = s[1]
                    n, _ = unit_size(units[u])
                    act.wait_ge(t_done, u + 1)
                    if u >= 2:
                        act.wait_ge(av_done, u - 1)
                    act.activation(probsT[:, u % 2, 0:n], PTb[:, 0:n], ACT.Copy).then_inc(pt_done, 1)

            for t in range(T):
                act.wait_ge(*freed(ticket_of[("out", "W1", t)]))
                act.wait_ge(sq_done, squares[0])
                squares[0] += 1
                act.activation(junkf[:, :], h[:, t, :], ACT.Square, accum_out=stat[:, 16 + t:17 + t]).then_inc(sq_done, 1)
            roots += 1
            act.wait_ge(var_done, roots)
            act.activation(stat[:, 16:20], stat[:, 16:20], ACT.Sqrt).then_inc(root_done, 1)
            act.wait_ge(late_in, 16 * LATE)
            act.activation(bb[:, :], bb_raw[:, :], ACT.Copy).then_inc(bb_hi, 1)
            for t in range(T):
                act.wait_ge(hs_ready, t + 1)
                act.dma_start(xn_rows[t * P:(t + 1) * P, :], hs[:, t, :]).then_inc(hs_stored, 16)
            for t in range(T):
                key = ("hn", t, 0)
                act.wait_ge(ticket_done, ticket_of[key] + 1)
                act.activation(hnT[:, 0:4, t * P:(t + 1) * P],
                               bank(key)[:, :].rearrange("p (k n) -> p k n", n=P), ACT.Copy).then_inc(free_a, 1)
            act.wait_ge(sub_done, 1)
            act.activation(gk[:, :, :], gk[:, :, :], ACT.Exp).then_inc(gexp_done, 1)

            def esplit(cc, n):
                slot = (NF + cc) % RING
                act.wait_ge(moe_in[cc % RAW], n * (2 * 32) + 32 * (cc // RAW + 1))
                act.wait_ge(used, n * CH + (NU + cc - RING + 1))
                act.activation(hi[:, slot, :], raw_moe[:, cc % RAW, :], ACT.Copy).then_inc(hi_ready, 1)

            def sigmoid(half, n):
                act.wait_ge(g_ready, n * 2 + half + 1)
                act.activation(s_sb[:, half, :], g_sb[:, half, :], ACT.Sigmoid, scale=ALPHA).then_inc(sig_ready, 1)

            def hidden_hi(half, n):
                act.wait_ge(ht_turned, n * 2 + half + 1)
                act.activation(hT_hi[:, 4 * half:4 * half + 4, :],
                               OB[:, :].rearrange("p (k n) -> p k n", n=P), ACT.Copy).then_inc(ht_hi, 1)

            def x_hi(par, r, n):
                act.wait_ge(xt_turned, n * 2 + r + 1)
                act.activation(exT_hi[:, par, 4 * r:4 * r + 4, :],
                               PTb[:, :].rearrange("p (k n) -> p k n", n=P), ACT.Copy).then_inc(xt_hi, 1)

            def y_copy(n):
                act.wait_ge(used, n * CH + (NU + CH))
                act.wait_ge(y_stored, n * 16 + 16)
                act.activation(y_sb[:, 0:512], SC[0][:, :], ACT.Copy).then_inc(y_ready, 1)
                act.activation(y_sb[:, 512:1024], SC[1][:, :], ACT.Copy).then_inc(y_ready, 1)

            def body(n, par, ahead):
                for cc in range(RING, 6):
                    esplit(cc, n)
                sigmoid(0, n)
                for cc in range(6, 9):
                    esplit(cc, n)
                hidden_hi(0, n)
                esplit(9, n)
                esplit(10, n)
                sigmoid(1, n)
                if ahead:
                    x_hi(1 - par, 0, n + 1)
                esplit(11, n)
                hidden_hi(1, n)
                if ahead:
                    x_hi(1 - par, 1, n + 1)
                    for cc in range(RING):
                        esplit(cc, n + 1)
                y_copy(n)

            x_hi(0, 0, 0)
            x_hi(0, 1, 0)
            for cc in range(RING):
                esplit(cc, 0)
            with act.Fori(0, NE // 2 - 1) as i:
                for par in range(2):
                    body(i * 2 + par, par, True)
            body(NE - 2, 0, True)
            body(NE - 1, 1, False)
            act.wait_ge(list_ready, 1)
            n_over = act.value_load(over_n[0:1, 0:1], min_val=0, max_val=MAX_OVER)
            with act.Fori(0, MAX_OVER) as j:
                with act.If(j < n_over):
                    x_hi(0, 0, j + NE)
                    x_hi(0, 1, j + NE)
                    for cc in range(RING):
                        esplit(cc, j + NE)
                    body(j + NE, 0, False)
            for t in range(T):
                act.wait_ge(h_final, t + 1)
                if t:
                    act.wait_ge(fsq, t)
                act.activation(junk2[:, :], h[:, t, :], ACT.Square, accum_out=stat[:, 20 + t:21 + t]).then_inc(fsq, 1)
                act.wait_ge(fvar, t + 1)
                act.activation(stat[:, 24 + t:25 + t], stat[:, 24 + t:25 + t], ACT.Sqrt).then_inc(froot, 1)

        @block.tensor
        def _(pe):
            def product(ps, parts, w_hi, w_lo, first, last):
                pe.matmul(ps, parts[0], w_hi, start=first, stop=False)
                pe.matmul(ps, parts[0], w_lo, start=False, stop=False)
                return pe.matmul(ps, parts[1], w_hi, start=False, stop=last)

            def lhs_of(name, oi, k):
                t = panels[name]["outs"][oi][0]
                cols = slice(t * P, (t + 1) * P)
                if name in ("MK", "MV"):
                    return memT_hi[:, k, cols], memT_lo[:, k, cols]
                if name == "UQ":
                    return cT_hi[:, k, cols], cT_lo[:, k, cols]
                if name == "UKV":
                    return cT_hi[:, 2, cols], cT_lo[:, 2, cols]
                if name[0] == "O":
                    return attT_hi[:, k, cols], attT_lo[:, k, cols]
                if name[0] == "W":
                    return mT_hi[:, k, cols], mT_lo[:, k, cols]
                return xT_hi[:, k, cols], xT_lo[:, k, cols]

            def lhs_ready(name, oi):
                t = panels[name]["outs"][oi][0]
                if name in ("MK", "MV"):
                    key = ("turn", "mem", t, 1)
                elif name in ("UQ", "UKV"):
                    key = ("turn", "c", t)
                elif name[0] == "O":
                    key = ("turn", "att", int(name[1]), t)
                elif name[0] == "W":
                    key = ("turn", "m", t, 1)
                else:
                    key = ("turn", "x", t, 1)
                pe.wait_ge(*freed(ticket_of[key]))

            def turn(s):
                kind = s[1]
                ps = take(pe, s)
                if kind in ("mem", "x"):
                    i = s[2] + (M if kind == "x" else 0)
                    pe.wait_ge(normed, i + 1)
                    for j in range(4):
                        k = 4 * s[3] + j
                        last = pe.transpose(ps[:, j * P:(j + 1) * P], rows[:, i, k * P:(k + 1) * P], ident[:, :])
                elif kind == "c":
                    pe.wait_ge(normed, M + T + s[2] + 1)
                    for j in range(3):
                        last = pe.transpose(ps[:, j * P:(j + 1) * P], cqr[:, s[2], j * P:(j + 1) * P], ident[:, :])
                elif kind == "kx":
                    pe.wait_ge(*freed(ticket_of[("out", "MK", 1)]))
                    for j in range(2):
                        for m in range(M):
                            hh = 2 * s[2] + j
                            last = pe.transpose(ps[:, (2 * j + m) * P:(2 * j + m + 1) * P],
                                                kmr[:, m, hh * P:(hh + 1) * P], ident[:, :])
                elif kind in ("qm", "km"):
                    pe.wait_ge(row_ready, 1 + 8)
                    if kind == "km":
                        pe.wait_ge(row_k, 8)
                    for t in range(T):
                        last = pe.transpose(ps[0:QK, t * P:(t + 1) * P], (qm if kind == "qm" else km)[:, t, s[2], :],
                                            ident[:, :])
                elif kind == "qs":
                    pe.wait_ge(row_ready, 9 + 4)
                    for t in range(T):
                        last = pe.transpose(ps[:, t * P:(t + 1) * P], rowsB[:, t, s[2] * P:(s[2] + 1) * P], ident[:, :])
                elif kind == "ks":
                    pe.wait_ge(row_ready, 9 + 8)
                    for t in range(T):
                        last = pe.transpose(ps[:, t * P:(t + 1) * P], ks_row[:, t, :], ident[:, :])
                elif kind == "qx":
                    pe.wait_ge(*freed(ticket_of[("out", "P3", T - 1)]))
                    for t in range(T):
                        last = pe.transpose(ps[:, t * P:(t + 1) * P], rowsB[:, t, s[2] * P:(s[2] + 1) * P], ident[:, :])
                elif kind == "att":
                    src = (att_mla, att_swa, att_xa)[s[2]]
                    pe.wait_ge(o_done, (32, 64, 80)[s[2]])
                    for j in range(4):
                        last = pe.transpose(ps[:, j * P:(j + 1) * P], src[:, s[3], j * P:(j + 1) * P], ident[:, :])
                elif kind == "m":
                    pe.wait_ge(*freed(ticket_of[("out", "O21", T - 1)]))
                    for j in range(4):
                        k = 4 * s[3] + j
                        last = pe.transpose(ps[:, j * P:(j + 1) * P], merged[:, s[2], k * P:(k + 1) * P], ident[:, :])
                last.then_inc(ticket_done, 1)

            def multiply(s):
                _, name, ci, oi = s
                p = panels[name]
                _, col, n = p["outs"][oi]
                c, per = p["ids"][ci], p["per"]
                key = ("out", name, oi)
                first, final = ci == 0, ci == len(p["ids"]) - 1
                ps = (take(pe, key) if first else bank(key))[:, 0:n]
                lhs_ready(name, oi)
                pe.wait_ge(lo_ready, c + 1)
                width = p["n"]
                bias = name[0] == "G"
                for k in range(per):
                    w = slice(k * width + col, k * width + col + n)
                    last = product(ps, lhs_of(name, oi, ci * per + k), hi[:, c % RING, w], lo[:, c % RING, w],
                                   first and k == 0, final and k == per - 1 and not bias)
                if oi == len(p["outs"]) - 1 and not final:
                    last.then_inc(used, 1)
                if final and bias:
                    pe.wait_ge(sel_ready, int(name[1]) * 2 + int(name[2]) + 1)
                    last = pe.matmul(ps, sel[:, :], bg[:, :], start=False, stop=True)
                if final:
                    last.then_inc(ticket_done, 1)

            def scores(u):
                kind, hh, qt = units[u]
                n, _ = unit_size(units[u])
                ps = SC[u % 2]
                if u >= 2:
                    pe.wait_ge(exp_done, u - 1)
                q = slice(qt * P, (qt + 1) * P)
                if kind == "mla":
                    pe.wait_ge(*freed(ticket_of[("turn", "km", hh)]))
                    pe.matmul(ps[:, 0:n], qT[0:QK, hh, q], kT[0:QK, hh, 0:n], start=True, stop=True)
                    last = pe.matmul(ps[:, n - P:n], ident_h[:, :], mask_cur[:, :], start=False, stop=True,
                                     skip_group_check=True)
                elif kind == "swa":
                    g, j = hh // GRP, hh % GRP
                    r = slice(SD * g, SD * (g + 1))
                    pe.wait_ge(*freed(ticket_of[("turn", "ks", 0)]))
                    pe.matmul(ps[:, 0:n], qsT[r, j, q], ksT[r, (qt + 1) * P - n:(qt + 1) * P], start=True, stop=True)
                    if qt:
                        pe.matmul(ps[:, 0:P], ident_h[:, :], mask_prev[:, :], start=False, stop=True,
                                  skip_group_check=True)
                    last = pe.matmul(ps[:, n - P:n], ident_h[:, :], mask_cur[:, :], start=False, stop=True,
                                     skip_group_check=True)
                else:
                    pe.wait_ge(*freed(ticket_of[("turn", "qx", hh)]))
                    last = pe.matmul(ps[:, 0:n], qxT[:, hh, q], kxT[:, hh, :], start=True, stop=True)
                last.then_inc(s_done, 1)

            def turn_probs(u):
                n, _ = unit_size(units[u])
                pe.wait_ge(exp_done, u + 1)
                pe.wait_ge(pt_done, u)
                for j in range(n // P):
                    last = pe.transpose(PTb[:, j * P:(j + 1) * P], probs[:, u % 2, j * P:(j + 1) * P], ident[:, :])
                last.then_inc(t_done, 1)

            def times_v(u):
                kind, hh, qt = units[u]
                n, _ = unit_size(units[u])
                pe.wait_ge(pt_done, u + 1)
                pe.wait_ge(o_done, u)
                blocks = n // P
                for j in range(blocks):
                    kb = j + (qt + 1 - blocks if kind == "swa" else 0)
                    v = {"mla": lambda: vm[:, kb, hh * VD:(hh + 1) * VD],
                         "swa": lambda: vs[:, kb, (hh // GRP) * SD:(hh // GRP + 1) * SD],
                         "xa": lambda: vx[:, kb, hh * XD:(hh + 1) * XD]}[kind]()
                    last = pe.matmul(OB[:, 0:v.shape[-1]], probsT[:, u % 2, j * P:(j + 1) * P], v,
                                     start=(j == 0), stop=(j == blocks - 1))
                last.then_inc(av_done, 1)

            pe.wait_ge(consts, NCONST)
            pe.wait_ge(bg_ready, 1)
            for s in steps:
                if s[0] == "turn":
                    turn(s)
                elif s[0] == "mm":
                    multiply(s)
                elif s[0] == "S":
                    scores(s[1])
                elif s[0] == "T":
                    turn_probs(s[1])
                elif s[0] == "AV":
                    times_v(s[1])

            for t in range(T):
                pe.wait_ge(hs_ready, t + 1)
                for r in range(2):
                    ps = take(pe, ("hn", t, r))
                    for j in range(4):
                        k = 4 * r + j
                        last = pe.transpose(ps[:, j * P:(j + 1) * P], hs[:, t, k * P:(k + 1) * P], ident[:, :])
                    last.then_inc(ticket_done, 1)
            ps = take(pe, "logits")
            pe.wait_ge(late_in, 16 * LATE)
            for r in range(2):
                pe.wait_ge(*freed(ticket_of[("hn", T - 1, r)]))
            for t in range(T):
                for k in range(KT):
                    last = pe.matmul(ps[:, t * NE:(t + 1) * NE], hnT[:, k, t * P:(t + 1) * P], wr[:, k, :],
                                     start=(k == 0), stop=(k == KT - 1))
            last.then_inc(ticket_done, 1)
            pe.wait_ge(mask_ready, 1)
            ps = take(pe, "rank")
            for t in range(T):
                for tb in range(t + 1):
                    last = pe.matmul(ps[:, t * NE:(t + 1) * NE], (below if tb == t else ones)[:, :], msk[:, tb, :],
                                     start=(tb == 0), stop=(tb == t))
            last.then_inc(ticket_done, 1)
            ps = take(pe, "count")
            for t in range(T):
                last = pe.matmul(ps[0:NE, 0:P], msk[:, t, :], ones[:, :], start=(t == 0), stop=(t == T - 1))
            last.then_inc(ticket_done, 1)

            def pick_sum(e, n):
                pe.wait_ge(pick_ready, n + 1)
                for t in range(T):
                    last = pe.matmul(PTb[:, 0:1], picks[:, t, :], val_e[:, t, e],
                                     start=(t == 0), stop=(t == T - 1))
                last.then_inc(pick_summed, 1)

            def turn_x(r, n):
                pe.wait_ge(xg_in, n * 16 + 16)
                if r:
                    pe.wait_ge(xt_ready, n * 2 + 1)
                for j in range(4):
                    k = 4 * r + j
                    last = pe.transpose(PTb[:, j * P:(j + 1) * P], xg[:, k * P:(k + 1) * P], ident[:, :])
                last.then_inc(xt_turned, 1)

            def gate_up(cc, n, par):
                slot, half = (NF + cc) % RING, cc // 4
                pe.wait_ge(lo_ready, n * CH + (NF + cc + 1))
                for kk in range(2):
                    k = (cc % 4) * 2 + kk
                    x_h, x_l = exT_hi[:, par, k, :], exT_lo[:, par, k, :]
                    w = [slice(kk * 1024 + s_ * 512, kk * 1024 + (s_ + 1) * 512) for s_ in range(2)]
                    for part, first in ((hi, k == 0), (lo, False)):
                        for s_ in range(2):
                            pe.matmul(PA[2 * half + s_][:, :], x_h, part[:, slot, w[s_]], start=first, stop=False)
                    for s_ in range(2):
                        last = pe.matmul(PA[2 * half + s_][:, :], x_l, hi[:, slot, w[s_]], start=False, stop=False)
                last.then_inc(used, 1)

            def biases(half, n):
                pe.wait_ge(sel_ready, n + 7)
                for s_ in range(2):
                    col = s_ * DE + half * HALF
                    last = pe.matmul(PA[2 * half + s_][:, :], sel[:, :], bb[:, col:col + HALF], start=False, stop=True)
                last.then_inc(gu_done, 1)

            def turn_hidden(half, n):
                pe.wait_ge(hid_ready, n * 2 + half + 1)
                for j in range(4):
                    last = pe.transpose(OB[:, j * P:(j + 1) * P], h_sb[:, half, j * P:(j + 1) * P], ident[:, :])
                last.then_inc(ht_turned, 1)

            def down(cc, n):
                slot = (NF + cc) % RING
                if cc == 8:
                    pe.wait_ge(ht_ready, n * 2 + 1)
                    pe.wait_ge(y_ready, n * 2 + 2)
                if cc == 10:
                    pe.wait_ge(ht_ready, n * 2 + 2)
                pe.wait_ge(lo_ready, n * CH + (NF + cc + 1))
                for kk in range(2):
                    k = (cc - 8) * 2 + kk
                    w = [slice(kk * 1024 + s_ * 512, kk * 1024 + (s_ + 1) * 512) for s_ in range(2)]
                    for part, first in ((hi, k == 0), (lo, False)):
                        for s_ in range(2):
                            pe.matmul(SC[s_][:, :], hT_hi[:, k, :], part[:, slot, w[s_]], start=first, stop=False)
                    for s_ in range(2):
                        last = pe.matmul(SC[s_][:, :], hT_lo[:, k, :], hi[:, slot, w[s_]], start=False, stop=(k == KT - 1))
                last.then_inc(used, 1)

            def body(n, par, ahead):
                pe.wait_ge(xt_ready, n * 2 + 2)
                gate_up(0, n, par)
                if ahead:
                    pick_sum(bass.ds(n + 1, 1), n + 1)
                for cc in range(1, 4):
                    gate_up(cc, n, par)
                biases(0, n)
                gate_up(4, n, par)
                gate_up(5, n, par)
                turn_hidden(0, n)
                gate_up(6, n, par)
                gate_up(7, n, par)
                biases(1, n)
                if ahead:
                    turn_x(0, n + 1)
                down(8, n)
                down(9, n)
                turn_hidden(1, n)
                if ahead:
                    turn_x(1, n + 1)
                down(10, n)
                down(11, n)

            pe.wait_ge(pt_done, U)
            pe.wait_ge(o_done, U)
            pick_sum(slice(0, 1), 0)
            pe.wait_ge(over_ready, 1)
            ps = take(pe, "ends")
            pe.matmul(ps[:, 0:NE], over[:, :], upto32[:, :], start=True, stop=True).then_inc(ticket_done, 1)
            pe.wait_ge(gd_ready, 1)
            ps = take(pe, "GT")
            for t in range(T):
                last = pe.transpose(ps[0:NE, t * P:(t + 1) * P], gdense[:, t, :], ident[:, :])
            last.then_inc(ticket_done, 1)
            pe.wait_ge(gt_ready, 1)
            for t in range(T):
                for hf in range(2):
                    ps = take(pe, ("bias", t, hf))
                    pe.matmul(ps[:, :], GT[:, t * P:(t + 1) * P], bdn[:, hf * 512:(hf + 1) * 512],
                              start=True, stop=True).then_inc(ticket_done, 1)
            turn_x(0, 0)
            turn_x(1, 0)
            pe.wait_ge(bb_ready, 1)
            pe.wait_ge(*freed(len(owner) - 1))

            with pe.Fori(0, NE // 2 - 1) as i:
                for par in range(2):
                    body(i * 2 + par, par, True)
            body(NE - 2, 0, True)
            body(NE - 1, 1, False)
            pe.wait_ge(list_ready, 1)
            n_over = pe.value_load(over_n[0:1, 0:1], min_val=0, max_val=MAX_OVER)
            with pe.Fori(0, MAX_OVER) as j:
                with pe.If(j < n_over):
                    e = pe.value_load(over_ei[0:1, bass.ds(j, 1)], min_val=0, max_val=NE - 1)
                    pick_sum(bass.ds(e, 1), j + NE)
                    turn_x(0, j + NE)
                    turn_x(1, j + NE)
                    body(j + NE, 0, False)

        @block.vector
        def _(dve):
            chain = [0]

            def link(ins):
                chain[0] += 1
                ins.then_inc(dve_chain, 1)
                dve.wait_ge(dve_chain, chain[0])

            def split(c):
                per, n = chunks[c][5], chunks[c][3]
                dve.wait_ge(hi_ready, c + 1)
                dve.tensor_tensor(lo[:, c % RING, 0:per * n], raw[:, c % RING, 0:per * n],
                                  hi[:, c % RING, 0:per * n].bitcast(F32), ALU.subtract).then_inc(lo_ready, 1)

            def rope(src, heads, half, freq, t, dst1, dst2, free, ready):
                s4 = src.rearrange("p h (a d) -> p h a d", a=2)
                n = heads * 2 * half
                A = ropeA[:, 0:n].rearrange("p (h a d) -> p h a d", h=heads, a=2)
                B = ropeB[:, 0:n].rearrange("p (h a d) -> p h a d", h=heads, a=2)
                c = cosv[:, t, freq:freq + half].unsqueeze(1).unsqueeze(1).to_broadcast([P, heads, 2, half])
                s_ = sinv[:, t, freq:freq + half].unsqueeze(1).unsqueeze(1).to_broadcast([P, heads, 2, half])
                link(dve.tensor_tensor(A, s4, c, ALU.mult))
                ins = dve.tensor_tensor(B, s4, s_, ALU.mult)
                link(ins)
                if free:
                    dve.sem_inc(free_v, 1)
                dve.tensor_tensor(dst1, A[:, :, 0, :], B[:, :, 1, :], ALU.subtract).then_inc(dve_chain, 1)
                chain[0] += 1
                last = dve.tensor_tensor(dst2, A[:, :, 1, :], B[:, :, 0, :], ALU.add)
                link(last)
                if ready:
                    dve.sem_inc(row_ready, 1)

            def variance(a, b, width):
                return dve.tensor_scalar(stat[:, a:b], stat[:, a:b], 1.0 / width, EPS, ALU.mult, ALU.add)

            dve.wait_ge(pos_in, 16)
            dve.wait_ge(consts, NCONST)
            link(dve.tensor_copy(rowid_f[:, :], rowid_i[:, :]))
            link(dve.tensor_scalar(rowid[:, :], rowid_f[:, :], 32.0, -32.0, ALU.is_ge, ALU.mult))
            link(dve.tensor_tensor(rowid[:, :], rowid[:, :], rowid_f[:, :], ALU.add))
            link(dve.tensor_copy(posf[:, :], pos_i[:, :]))
            for t in range(T):
                link(dve.tensor_scalar(ang[:, t, :], inv_f[:, :], posf[:, t:t + 1], None, ALU.mult))
            link(dve.tensor_scalar(ang_k[:, :, :], ang[:, :, :], 1.0 / TWO_PI, ROUND, ALU.mult, ALU.add))
            link(dve.tensor_scalar(ang_k[:, :, :], ang_k[:, :, :], -ROUND, None, ALU.add))
            for part in (PI_A, PI_B, PI_C):
                link(dve.scalar_tensor_tensor(ang[:, :, :], ang_k[:, :, :], -part, ang[:, :, :], ALU.mult, ALU.add))
            ins = dve.tensor_scalar(ang[:, :, :], ang[:, :, :], PI_SAFE, -PI_SAFE, ALU.min, ALU.max)
            ins.then_inc(trig, 1)
            dve.wait_ge(trig, 1)
            link(dve.scalar_tensor_tensor(ang_k[:, :, :], ang[:, :, :], -1.0, ang[:, :, :], ALU.mult, ALU.min))
            dve.tensor_scalar(ang_k[:, :, :], ang_k[:, :, :], float(np.pi / 2), None, ALU.add).then_inc(trig, 1)
            dve.wait_ge(y_stored, 16)
            link(dve.tensor_scalar(nsink_b[:, :], sink_b[:, :], -1.0, None, ALU.mult))
            dve.wait_ge(bg_hi, 1)
            dve.tensor_tensor(bg[32:64, :], bg_raw[32:64, :], bg[32:64, :].bitcast(F32), ALU.subtract).then_inc(bg_ready, 1)
            for c in range(RING):
                split(c)

            n_part, n_sq, roots, n_row = 0, 0, 0, 0
            gates_before = None
            for s in steps:
                if s[0] == "norm":
                    roots += 1
                    if s[1] < 2:
                        a, b = ((0, M), (M, M + T))[s[1]]
                        n_sq += b - a
                        dve.wait_ge(sq_done, n_sq)
                        variance(a, b, D).then_inc(var_done, 1)
                        dve.wait_ge(root_done, roots)
                        link(dve.reciprocal(stat[:, a:b], stat[:, a:b]))
                        dve.wait_ge((gmem_in, gmix_in)[s[1]], 16)
                        for i in range(a, b):
                            dve.wait_ge(rows_in[i], 16)
                            dve.scalar_tensor_tensor(rows[:, i, :], rows[:, i, :], stat[:, i:i + 1],
                                                     (gmem_b, gmix_b)[s[1]][:, :], ALU.mult, ALU.mult).then_inc(normed, 1)
                    else:
                        link(variance(8, 12, QR))
                        variance(12, 16, KVR).then_inc(var_done, 1)
                        dve.wait_ge(root_done, roots)
                        link(dve.reciprocal(stat[:, 8:16], stat[:, 8:16]))
                        dve.wait_ge(gq_in, 16)
                        dve.wait_ge(gkv_in, 16)
                        for t in range(T):
                            link(dve.scalar_tensor_tensor(cqr[:, t, 0:QR], cqr[:, t, 0:QR], stat[:, 8 + t:9 + t],
                                                          gq_b[:, :], ALU.mult, ALU.mult))
                            dve.scalar_tensor_tensor(cqr[:, t, QR:], cqr[:, t, QR:], stat[:, 12 + t:13 + t],
                                                     gkv_b[:, :], ALU.mult, ALU.mult).then_inc(normed, 1)
                        for t in range(T):
                            ins = dve.tensor_copy(km[:, t, :, NOPE:QK], krr[:, t, :].unsqueeze(1)
                                                  .to_broadcast([P, MLA_H, ROPE]))
                            if t < T - 1:
                                link(ins)
                        ins.then_inc(row_ready, 1)
                elif s[0] == "turn":
                    kind, n = s[1], ticket_of[s]
                    pb = bank(s)
                    if kind in ("mem", "x", "c", "att", "m"):
                        n_part += 1
                        dve.wait_ge(part_hi, n_part)
                        v = pb[:, :].rearrange("p (k n) -> p k n", n=P)
                        if kind == "mem":
                            a, b = slice(4 * s[3], 4 * s[3] + 4), slice(s[2] * P, (s[2] + 1) * P)
                            dst, hp = memT_lo[:, a, b], memT_hi[:, a, b]
                        elif kind == "x":
                            a, b = slice(4 * s[3], 4 * s[3] + 4), slice(s[2] * P, (s[2] + 1) * P)
                            dst, hp = xT_lo[:, a, b], xT_hi[:, a, b]
                        elif kind == "c":
                            b = slice(s[2] * P, (s[2] + 1) * P)
                            dst, hp, v = cT_lo[:, :, b], cT_hi[:, :, b], v[:, 0:3, :]
                        elif kind == "att":
                            b = slice(s[3] * P, (s[3] + 1) * P)
                            dst, hp = attT_lo[:, :, b], attT_hi[:, :, b]
                        else:
                            a, b = slice(4 * s[3], 4 * s[3] + 4), slice(s[2] * P, (s[2] + 1) * P)
                            dst, hp = mT_lo[:, a, b], mT_hi[:, a, b]
                        if kind == "m":
                            dve.scalar_tensor_tensor(dst, v, 0.5, hp.bitcast(F32), ALU.mult, ALU.subtract).then_inc(free_v, 1)
                        else:
                            dve.tensor_tensor(dst, v, hp.bitcast(F32), ALU.subtract).then_inc(free_v, 1)
                    else:
                        dve.wait_ge(ticket_done, n + 1)
                        if kind == "kx":
                            dst, v = kxT[:, 2 * s[2]:2 * s[2] + 2, :], pb[:, :].rearrange("p (h n) -> p h n", h=2)
                        elif kind in ("qm", "km"):
                            dst, v = (qT if kind == "qm" else kT)[0:QK, s[2], :], pb[0:QK, :]
                        elif kind == "qs":
                            dst, v = qsT[:, s[2], :], pb[:, :]
                        elif kind == "ks":
                            dst, v = ksT[:, :], pb[:, :]
                        else:
                            dst, v = qxT[:, s[2], :], pb[:, :]
                        dve.tensor_copy(dst, v).then_inc(free_v, 1)
                elif s[0] == "mm":
                    _, name, ci, oi = s
                    p = panels[name]
                    final = ci == len(p["ids"]) - 1
                    key = ("out", name, oi)
                    ps = bank(key)
                    t = p["outs"][oi][0]
                    if name[0] == "G" and ci == 0 and oi == 0:
                        if gates_before is not None:
                            dve.wait_ge(*freed(ticket_of[("out", gates_before, T - 1)]))
                        gates_before = name
                        dve.tensor_scalar(sel[:, :], rowid[:, 0:1].to_broadcast([64, P]),
                                          float(int(name[1]) * 2 + int(name[2])), None, ALU.is_equal).then_inc(sel_ready, 1)
                    if final and name[0] != "G" and name != "UKV":
                        dve.wait_ge(ticket_done, ticket_of[key] + 1)
                        if name == "MK":
                            dve.tensor_copy(kmr[:, oi, :], ps[:, :]).then_inc(free_v, 1)
                        elif name == "MV":
                            dve.tensor_copy(vx[:, oi, :], ps[:, :]).then_inc(free_v, 1)
                        elif name == "P0":
                            n_sq += 2
                            dve.wait_ge(sq_done, n_sq)
                            link(dve.tensor_copy(cqr[:, t, :], ps[:, CQ:CKR]))
                            dve.wait_ge(trig_ready, 2)
                            rope(ps[:, CKR:CQS].rearrange("p (h d) -> p h d", h=1), 1, ROPE // 2, 32, t,
                                 krr[:, t, 0:ROPE // 2].unsqueeze(1), krr[:, t, ROPE // 2:].unsqueeze(1), True, False)
                        elif name == "UQ":
                            half = oi % 2
                            v = ps[:, 0:384].rearrange("p (h d) -> p h d", h=4)
                            q = qm[:, t, 4 * half:4 * half + 4, :]
                            link(dve.tensor_copy(q[:, :, 0:NOPE], v[:, :, 0:NOPE]))
                            rope(v[:, :, NOPE:QK], 4, ROPE // 2, 32, t, q[:, :, NOPE:NOPE + ROPE // 2],
                                 q[:, :, NOPE + ROPE // 2:QK], True, True)
                        elif name == "P1":
                            q = rowsB[:, t, :].rearrange("p (j g a d) -> p g j a d", j=GRP, g=SWA_KV, a=2)
                            v = ps[:, :].rearrange("p (g j d) -> p g j d", g=SWA_KV, j=GRP)
                            for g in range(SWA_KV):
                                rope(v[:, g], GRP, SD // 2, 0, t, q[:, g, :, 0, :], q[:, g, :, 1, :],
                                     g == SWA_KV - 1, g == SWA_KV - 1)
                        elif name == "P2":
                            link(dve.tensor_copy(vs[:, t, :], ps[:, P:2 * P]))
                            v = ps[:, 0:P].rearrange("p (g d) -> p g d", g=SWA_KV)
                            q = ks_row[:, t, :].rearrange("p (g a d) -> p g a d", g=SWA_KV, a=2)
                            rope(v, SWA_KV, SD // 2, 0, t, q[:, :, 0, :], q[:, :, 1, :], True, True)
                        elif name == "P3":
                            dve.tensor_copy(rowsB[:, t, :], ps[:, :]).then_inc(free_v, 1)
                        elif name[0] == "O":
                            b, hf = int(name[1]), int(name[2])
                            dve.wait_ge(*freed(ticket_of[("out", f"G{b}{hf}", t)]))
                            m = merged[:, t, hf * 512:(hf + 1) * 512]
                            if b == 0:
                                dve.scalar_tensor_tensor(m, gate[:, t, :], 1.0, ps[:, :], ALU.add, ALU.mult).then_inc(free_v, 1)
                            else:
                                gated = (ropeA, ropeB)[t % 2]
                                link(dve.scalar_tensor_tensor(gated[:, :], gate[:, t, :], 1.0, ps[:, :], ALU.add, ALU.mult))
                                dve.tensor_tensor(m, m, gated[:, :], ALU.add).then_inc(free_v, 1)
                        elif name[0] == "W":
                            hf = int(name[1])
                            dve.wait_ge(h_in, 16)
                            m = h[:, t, hf * 512:(hf + 1) * 512]
                            dve.tensor_tensor(m, m, ps[:, :], ALU.add).then_inc(free_v, 1)
                    if oi == len(p["outs"]) - 1 and p["ids"][ci] + RING < NF:
                        split(p["ids"][ci] + RING)
                elif s[0] == "S":
                    u = s[1]
                    kind, hh, _ = units[u]
                    n, scale = unit_size(units[u])
                    dve.wait_ge(s_done, u + 1)
                    link(dve.reduce_max(mx[:, u % 8:u % 8 + 1], SC[u % 2][:, 0:n], AX.X))
                    if kind == "swa":
                        dve.tensor_scalar(nmax[:, u:u + 1], mx[:, u % 8:u % 8 + 1], -scale, nsink_b[:, hh:hh + 1],
                                          ALU.mult, ALU.min).then_inc(nm_done, 1)
                    else:
                        dve.tensor_scalar(nmax[:, u:u + 1], mx[:, u % 8:u % 8 + 1], -scale, None,
                                          ALU.mult).then_inc(nm_done, 1)
                elif s[0] == "AV":
                    u = s[1]
                    kind, hh, qt = units[u]
                    width = XD if kind == "xa" else VD
                    dst = {"mla": att_mla, "swa": att_swa, "xa": att_xa}[kind][:, qt, hh * width:(hh + 1) * width]
                    dve.wait_ge(exp_done, u + 1)
                    r = rsum[:, u:u + 1]
                    if kind == "swa":
                        dve.wait_ge(es_done, u - 31)
                        link(dve.tensor_tensor(r, r, esink[:, u % 8:u % 8 + 1], ALU.add))
                    link(dve.reciprocal(r, r))
                    dve.wait_ge(av_done, u + 1)
                    dve.tensor_scalar(dst, OB[:, 0:width], r, None, ALU.mult).then_inc(o_done, 1)

            dve.wait_ge(sq_done, n_sq + T)
            roots += 1
            variance(16, 20, D).then_inc(var_done, 1)
            dve.wait_ge(root_done, roots)
            link(dve.reciprocal(stat[:, 16:20], stat[:, 16:20]))
            dve.wait_ge(late_in, 16 * LATE)
            for t in range(T):
                dve.scalar_tensor_tensor(hs[:, t, :], h[:, t, :], stat[:, 16 + t:17 + t], gffn_b[:, :],
                                         ALU.mult, ALU.mult).then_inc(hs_ready, 1)
            for t in range(T):
                key = ("hn", t, 1)
                dve.wait_ge(ticket_done, ticket_of[key] + 1)
                dve.tensor_copy(hnT[:, 4:8, t * P:(t + 1) * P],
                                bank(key)[:, :].rearrange("p (k n) -> p k n", n=P)).then_inc(free_v, 1)
            dve.wait_ge(ticket_done, ticket_of["logits"] + 1)
            ins = dve.tensor_tensor(lg[:, :, :], bank("logits")[:, 0:T * NE].rearrange("p (t e) -> p t e", t=T),
                                    br_b[:, :].unsqueeze(1).to_broadcast([P, T, NE]), ALU.add)
            ins.then_inc(free_v, 1)
            dve.wait_ge(*freed(ticket_of["logits"]))
            for t in range(T):
                link(dve.max(mval[:, t, :], lg[:, t, :]))
            for t in range(T):
                link(dve.max_index(midx[:, t, :], mval[:, t, :], lg[:, t, :]))
            dve.tensor_tensor(gk[:, :, :], mval[:, :, 0:TOPK], mval[:, :, 0:1].to_broadcast([P, T, TOPK]),
                              ALU.subtract).then_inc(sub_done, 1)
            link(dve.tensor_copy(idxf[:, :, :], midx[:, :, 0:TOPK]))
            dve.wait_ge(route_ready, 9)

            def over_experts(x):
                return x[:, :, :].unsqueeze(3).to_broadcast([P, T, TOPK, NE])

            def by_expert(x):
                return x[:, :, :, :].rearrange("p t k e -> p t e k")

            link(dve.tensor_tensor(onehot[:, :, :, :], over_experts(idxf),
                                   lanes_e[:, :].unsqueeze(1).unsqueeze(1).to_broadcast([P, T, TOPK, NE]), ALU.is_equal))
            dve.tensor_reduce(msk[:, :, :], by_expert(onehot), AX.X, ALU.add).then_inc(mask_ready, 1)
            link(dve.tensor_tensor(tmp512[:, :, :, :], onehot[:, :, :, :], over_experts(asg_f), ALU.mult))
            link(dve.tensor_reduce(val_e[:, :, :], by_expert(tmp512), AX.X, ALU.add))
            dve.wait_ge(ticket_done, ticket_of["rank"] + 1)
            dve.wait_ge(mask_ready, 1)
            ins = dve.scalar_tensor_tensor(rank_e[:, :, :], bank("rank")[:, 0:T * NE].rearrange("p (t e) -> p t e", t=T),
                                           1.0, msk[:, :, :], ALU.add, ALU.mult)
            ins.then_inc(free_v, 1)
            dve.wait_ge(*freed(ticket_of["rank"]))
            dve.tensor_scalar(rank_e[:, :, :], rank_e[:, :, :], -1.0, None, ALU.add).then_inc(mask_ready, 1)

            def find_rows(par, n, blocks_stored):
                dve.wait_ge(pick_summed, n + 1)
                dve.wait_ge(y_stored, blocks_stored * 16 + 16)
                p1 = PTb[:, 0:1]
                dve.tensor_scalar(idx_t[:, 0:1], p1, 0.0, NOWHERE, ALU.is_equal, ALU.mult).then_inc(find_chain, 1)
                dve.wait_ge(find_chain, n * 3 - 2)
                dve.scalar_tensor_tensor(idx_t[:, 1:2], p1, -1.0, idx_t[:, 0:1], ALU.add, ALU.add).then_inc(find_chain, 1)
                dve.wait_ge(find_chain, n * 3 - 1)
                dve.tensor_copy(asg_sb[:, par:par + 1], idx_t[:, 1:2]).then_inc(find_chain, 1)
                dve.wait_ge(find_chain, n * 3)
                dve.tensor_scalar(tok_sb[:, par:par + 1], asg_sb[:, par:par + 1], 2, None,
                                  ALU.logical_shift_right).then_inc(tok_ready, 1)

            dve.wait_ge(ticket_done, ticket_of["count"] + 1)
            cnt = bank("count")[0:NE, 0:P]
            link(dve.tensor_scalar(over[:, :], cnt, float(P), None, ALU.is_gt))
            link(dve.scalar_tensor_tensor(over[:, :], cnt, float(2 * P), over[:, :], ALU.is_gt, ALU.add))
            ins = dve.scalar_tensor_tensor(over[:, :], cnt, float(3 * P), over[:, :], ALU.is_gt, ALU.add)
            link(ins)
            dve.sem_inc(free_v, 1)
            dve.sem_inc(over_ready, 1)
            dve.wait_ge(pick_summed, 1)
            link(dve.tensor_scalar(idx_t[:, 0:1], PTb[:, 0:1], 0.0, NOWHERE, ALU.is_equal, ALU.mult))
            link(dve.scalar_tensor_tensor(idx_t[:, 1:2], PTb[:, 0:1], -1.0, idx_t[:, 0:1], ALU.add, ALU.add))
            link(dve.tensor_copy(asg_sb[:, 0:1], idx_t[:, 1:2]))
            dve.tensor_scalar(tok_sb[:, 0:1], asg_sb[:, 0:1], 2, None, ALU.logical_shift_right).then_inc(tok_ready, 1)
            dve.wait_ge(gexp_done, 1)
            gsum = mx[:, 0:T]
            link(dve.reduce_sum(gsum, gk[:, :, :], AX.X))
            link(dve.reciprocal(gsum, gsum))
            link(dve.tensor_tensor(gk[:, :, :], gk[:, :, :], gsum.unsqueeze(2).to_broadcast([P, T, TOPK]), ALU.mult))
            link(dve.tensor_tensor(tmp512[:, :, :, :], onehot[:, :, :, :], over_experts(gk), ALU.mult))
            dve.tensor_reduce(gdense[:, :, :], by_expert(tmp512), AX.X, ALU.add).then_inc(gd_ready, 1)
            dve.wait_ge(ticket_done, ticket_of["ends"] + 1)
            link(dve.tensor_copy(ends[:, :], bank("ends")[:, 0:NE]))
            dve.sem_inc(free_v, 1)
            dve.wait_ge(gd_ready, 1)
            is_past = tmp512[:, :, :, :].rearrange("p t k e -> p (t k) e")
            past_end = onehot[:, :, :, :].rearrange("p t k e -> p (t k) e")
            ends_b = ends[:, :].unsqueeze(1).to_broadcast([P, MAX_OVER, NE])
            link(dve.tensor_tensor(is_past, ends_b, over_i[:, :, :], ALU.is_le))
            link(dve.tensor_tensor(past_end, is_past, ends_b, ALU.mult))
            link(dve.tensor_reduce(over_e[:, :], is_past, AX.X, ALU.add))
            link(dve.tensor_reduce(over_b[:, :], past_end, AX.X, ALU.max))
            link(dve.tensor_scalar(over_e[:, :], over_e[:, :], float(NE - 1), None, ALU.min))
            link(dve.scalar_tensor_tensor(over_b[:, :], over_b[:, :], -1.0, over_i[:, :, 0], ALU.mult, ALU.add))
            link(dve.tensor_scalar(over_b[:, :], over_b[:, :], 1.0, float(P), ALU.add, ALU.mult))
            link(dve.tensor_copy(over_ei[:, :], over_e[:, :]))
            link(dve.tensor_copy(ecol[:, NE:], over_e[0:64, :]))
            dve.tensor_copy(over_n[:, :], ends[0:1, NE - 1:NE]).then_inc(list_ready, 1)
            dve.wait_ge(ticket_done, ticket_of["GT"] + 1)
            ins = dve.tensor_copy(GT[:, :], bank("GT")[0:NE, :])
            link(ins)
            dve.sem_inc(free_v, 1)
            dve.sem_inc(gt_ready, 1)
            dve.wait_ge(bb_hi, 1)
            dve.tensor_tensor(bb[32:64, :], bb_raw[32:64, :], bb[32:64, :].bitcast(F32), ALU.subtract).then_inc(bb_ready, 1)
            for t in range(T):
                for hf in range(2):
                    key = ("bias", t, hf)
                    dve.wait_ge(ticket_done, ticket_of[key] + 1)
                    m = h[:, t, hf * 512:(hf + 1) * 512]
                    dve.tensor_tensor(m, m, bank(key)[:, :], ALU.add).then_inc(free_v, 1)

            def esplit(cc, n):
                slot = (NF + cc) % RING
                dve.wait_ge(hi_ready, n * CH + (NF + cc + 1))
                dve.tensor_tensor(lo[:, slot, :], raw_moe[:, cc % RAW, :], hi[:, slot, :].bitcast(F32),
                                  ALU.subtract).then_inc(lo_ready, 1)

            def x_lo(par, r, n):
                dve.wait_ge(xt_hi, n * 2 + r + 1)
                a = slice(4 * r, 4 * r + 4)
                dve.tensor_tensor(exT_lo[:, par, a, :], PTb[:, :].rearrange("p (k n) -> p k n", n=P),
                                  exT_hi[:, par, a, :].bitcast(F32), ALU.subtract).then_inc(xt_ready, 1)

            def swiglu(half, n):
                dve.wait_ge(gu_done, n * 2 + half + 3)
                dve.tensor_scalar(g_sb[:, half, :], PA[2 * half][:, :], LIMIT, None, ALU.min).then_inc(g_ready, 1)
                dve.tensor_scalar(u_sb[:, half, :], PA[2 * half + 1][:, :], LIMIT, -LIMIT, ALU.min, ALU.max).then_inc(glu_chain, 1)
                dve.wait_ge(glu_chain, n * 4 + (2 * half + 1))
                dve.wait_ge(g_ready, n * 2 + half + 1)
                dve.scalar_tensor_tensor(u_sb[:, half, :], u_sb[:, half, :], 1.0, g_sb[:, half, :],
                                         ALU.add, ALU.mult).then_inc(glu_chain, 1)
                dve.wait_ge(glu_chain, n * 4 + (2 * half + 2))
                dve.wait_ge(sig_ready, n * 2 + half + 1)
                dve.tensor_tensor(h_sb[:, half, :], u_sb[:, half, :], s_sb[:, half, :], ALU.mult).then_inc(hid_ready, 1)

            def hidden_lo(half, n):
                dve.wait_ge(ht_hi, n * 2 + half + 1)
                a = slice(4 * half, 4 * half + 4)
                dve.tensor_tensor(hT_lo[:, a, :], OB[:, :].rearrange("p (k n) -> p k n", n=P),
                                  hT_hi[:, a, :].bitcast(F32), ALU.subtract).then_inc(ht_ready, 1)

            def select(n):
                dve.wait_ge(gu_done, n * 2 + 2)
                dve.tensor_scalar(sel[:, :], ecol[:, bass.ds(n, 1)].to_broadcast([64, P]), rowid[:, 0:1], None,
                                  ALU.is_equal).then_inc(sel_ready, 1)

            def body(n, par, ahead):
                select(n)
                esplit(3, n)
                esplit(4, n)
                if ahead:
                    find_rows(1 - par, n + 1, n)
                esplit(5, n)
                swiglu(0, n)
                for cc in range(6, 9):
                    esplit(cc, n)
                hidden_lo(0, n)
                esplit(9, n)
                swiglu(1, n)
                esplit(10, n)
                if ahead:
                    x_lo(1 - par, 0, n + 1)
                esplit(11, n)
                hidden_lo(1, n)
                if ahead:
                    x_lo(1 - par, 1, n + 1)
                    for cc in range(RING):
                        esplit(cc, n + 1)

            x_lo(0, 0, 0)
            x_lo(0, 1, 0)
            for cc in range(RING):
                esplit(cc, 0)
            with dve.Fori(0, NE // 2 - 1) as i:
                for par in range(2):
                    body(i * 2 + par, par, True)
            body(NE - 2, 0, True)
            body(NE - 1, 1, False)
            n_over = dve.value_load(over_n[0:1, 0:1], min_val=0, max_val=MAX_OVER)
            with dve.Fori(0, MAX_OVER) as j:
                with dve.If(j < n_over):
                    e = dve.value_load(over_ei[0:1, bass.ds(j, 1)], min_val=0, max_val=NE - 1)
                    dve.wait_ge(pick_ready, j + NE)
                    dve.tensor_scalar(rank_o[:, :], rank_e[:, :, bass.ds(e, 1)].rearrange("p t o -> p (t o)"),
                                      over_b[:, bass.ds(j, 1)], None, ALU.subtract).then_inc(shift_ready, 1)
                    find_rows(0, j + NE, j + NE)
                    x_lo(0, 0, j + NE)
                    x_lo(0, 1, j + NE)
                    for cc in range(RING):
                        esplit(cc, j + NE)
                    body(j + NE, 0, False)

            def finish(t):
                dve.wait_ge(fsq, t + 1)
                dve.tensor_scalar(stat[:, 24 + t:25 + t], stat[:, 20 + t:21 + t], 1.0 / D, EPS,
                                  ALU.mult, ALU.add).then_inc(fvar, 1)
                dve.wait_ge(froot, t + 1)
                link(dve.reciprocal(stat[:, 24 + t:25 + t], stat[:, 24 + t:25 + t]))
                dve.scalar_tensor_tensor(fin[:, t, :], h[:, t, :], stat[:, 24 + t:25 + t], gfin_b[:, :],
                                         ALU.mult, ALU.mult).then_inc(fin_ready, 1)

            for t in range(T):
                dve.wait_ge(yk_in[t], 16)
                for k in range(TOPK):
                    ins = dve.scalar_tensor_tensor(h[:, t, :], yk[:, t, k, :], gk[:, t, k:k + 1], h[:, t, :],
                                                   ALU.mult, ALU.add)
                    if k < TOPK - 1:
                        link(ins)
                ins.then_inc(h_final, 1)
                dve.wait_ge(h_final, t + 1)
                if t:
                    finish(t - 1)
            finish(T - 1)


_INS = ["x", "mem", "positions", "g_mix", "w_in", "g_mla_q", "w_mla_uq", "g_mla_kv", "w_mla_ukv", "w_mla_o",
        "swa_sinks", "w_swa_o", "g_mem", "w_mem_kv", "w_xa_o", "b_gate", "w_out", "g_ffn", "w_router",
        "b_router", "w_gate_up", "b_gate_up", "w_down", "b_down", "g_final"]


def kernel(**inputs):
    import numpy as _np
    import concourse.bacc as _bacc
    from concourse import mybir as _mybir
    from concourse.bass_utils import run_bass_kernel_spmd as _run

    nc = _bacc.Bacc("TRN2", target_bir_lowering=False, num_devices=1)
    arrays, args = {}, []
    for name in _INS:
        a = _np.ascontiguousarray(inputs[name])
        arrays[f"in_{name}"] = a
        args.append(nc.dram_tensor(f"in_{name}", a.shape, _mybir.dt.from_np(a.dtype), kind="ExternalInput").ap())
    out = nc.dram_tensor("out", (1, SEQ, D), F32, kind="ExternalOutput").ap()
    build_layer(nc, *args, out)
    r = _run(nc, [arrays], core_ids=[0])
    return r.results[0]["out"]
```

```python
from contextlib import ExitStack

import numpy as np
import concourse.bass as bass
from concourse import mybir

P = 128
ALU = mybir.AluOpType
ACT = mybir.ActivationFunctionType
AX = mybir.AxisListType
F32 = mybir.dt.float32
F32R = mybir.dt.float32r
BF16 = mybir.dt.bfloat16
I32 = mybir.dt.int32
U32 = mybir.dt.uint32

D = 1024
SEQ = 512
MEM = 256
T = SEQ // P
M = MEM // P
KT = D // P
EPS = 1e-6
THETA = 10000.0
MLA_H, NOPE, ROPE, VD = 8, 64, 32, 64
QK = NOPE + ROPE
QR, KVR = 256, 128
SWA_H, SWA_KV, SD = 8, 2, 64
GRP = SWA_H // SWA_KV
XA_H, XD = 4, 128
NE, TOPK, DE = 32, 4, 1024
ALPHA, LIMIT = 1.702, 7.0
HALF = DE // 2
CQ, CKV, CKR = 0, QR, QR + KVR
CQS = CKR + ROPE
CKS = CQS + SWA_H * SD
CVS = CKS + SWA_KV * SD
CQX = CVS + SWA_KV * SD
CG = CQX + XA_H * XD
NEG = -1e30
ROUND = 1.5 * 2.0 ** 23
TWO_PI = 2.0 * float(np.pi)
PI_A = 6.28125
PI_B = float(np.float32(TWO_PI - PI_A))
PI_C = float(TWO_PI - PI_A - PI_B)
PI_SAFE = 3.1415925
NOWHERE = float(2 ** 22)
MAX_OVER = 16
CH = 12
RING = 3
ERING = 4
RAW = 8


BY_SCALAR = ("qs", "ks", "qx")


def make_plan():
    panels, chunks, steps = {}, [], []

    def panel(name, weight, col, n, kt, per, outs):
        ids = []
        for k0 in range(0, kt, per):
            ids.append(len(chunks))
            chunks.append((name, weight, col, n, k0, per))
        panels[name] = dict(ids=ids, per=per, n=n, outs=outs)

    def mm(name):
        p = panels[name]
        return [("mm", name, ci, oi) for ci in range(len(p["ids"])) for oi in range(len(p["outs"]))]

    HALVED = ["P1", "P2", "P3"] + [f"{g}{b}{hf}" for g in "GO" for b in range(2) for hf in range(2)]
    panel("MK", "w_mem_kv", 0, 512, KT, 4, [(m, 0, 512) for m in range(M)])
    panel("P0", "w_in", 0, CQS, KT, 4, [(t, 0, CQS) for t in range(T)])
    panel("MV", "w_mem_kv", 512, 512, KT, 4, [(m, 0, 512) for m in range(M)])
    panel("UQ", "w_mla_uq", 0, MLA_H * QK, QR // P, 2, [(t, h * 384, 384) for t in range(T) for h in range(2)])
    panel("UKV", "w_mla_ukv", 0, 1024, 1, 1, [(t, h * 512, 512) for t in range(T) for h in range(2)])
    panel("P1", "w_in", CQS, 512, KT, 4, [(t, 0, 512) for t in range(T)])
    panel("P2", "w_in", CKS, 256, KT, 8, [(t, 0, 256) for t in range(T)])
    panel("P3", "w_in", CQX, 512, KT, 4, [(t, 0, 512) for t in range(T)])
    outw = ["w_mla_o", "w_swa_o", "w_xa_o"]
    for b in range(3):
        for hf in range(2):
            panel(f"G{b}{hf}", "w_in", CG + b * D + hf * 512, 512, KT, 4, [(t, 0, 512) for t in range(T)])
            panel(f"O{b}{hf}", outw[b], hf * 512, 512, 4, 4, [(t, 0, 512) for t in range(T)])
    for hf in range(2):
        panel(f"W{hf}", "w_out", hf * 512, 512, KT, 4, [(t, 0, 512) for t in range(T)])

    units = [("mla", h, qt) for h in range(MLA_H) for qt in range(T)]
    units += [("swa", h, n) for h in range(SWA_H) for n in range(T)]
    units += [("xa", h, qt) for h in range(XA_H) for qt in range(T)]

    def attend(first, last, filler):
        filler = [x for s in filler for x in ([("begin", *s[1:]), s] if s[0] == "mm" and s[1] in HALVED else [s])]
        n = last - first + 2
        done = 0
        reached = [sum(1 if s[0] == "turn" else 3 for s in filler[:j + 1]) for j in range(len(filler))]
        for i in range(n):
            if first + i < last:
                steps.append(("S", first + i))
            if i >= 1 and first + i - 1 < last:
                steps.append(("T", first + i - 1))
            if i >= 2:
                steps.append(("AV", first + i - 2))
            upto = sum(1 for c in reached if c <= reached[-1] * (i + 1) // n)
            steps.extend(filler[done:upto])
            done = upto

    steps += [("square", i) for i in range(M)] + [("norm", 0), ("split", 0)]
    steps += [("turn", "mem", m, r) for m in range(M) for r in range(2)]
    steps += [("square", M), ("square", M + 1), ("split", 1), ("square", M + 2), ("square", M + 3)]
    steps += [("norm", 1), ("split", 2)]
    steps += mm("MK")
    steps += [("turn", "x", t, r) for t in range(T) for r in range(2)]
    steps.append(("angles",))
    steps += mm("P0")
    steps.append(("norm", 2))
    steps += mm("MV")
    steps += [("turn", "kx", j) for j in range(2)]
    steps.append(("keys",))
    steps += [("turn", "c", t) for t in range(T)]
    steps += mm("UQ") + mm("UKV")
    steps += [("turn", "qm", h) for h in range(MLA_H)] + [("turn", "km", h) for h in range(MLA_H)]
    fill = mm("P1") + mm("P2") + [("turn", "qs", j) for j in range(GRP)] + mm("P3")
    fill += [("turn", "ks", 0)] + [("turn", "qx", h) for h in range(XA_H)]
    attend(0, 32, fill)
    steps += [("turn", "att", 0, t) for t in range(T)]
    attend(32, 64, mm("G00") + mm("O00") + mm("G01") + mm("O01"))
    attend(64, 80, [("turn", "att", 1, t) for t in range(T)] + mm("G10") + mm("O10") + mm("G11") + mm("O11"))
    steps += [("turn", "att", 2, t) for t in range(T)]
    steps += mm("G20") + mm("O20") + mm("G21") + mm("O21")
    steps += [("turn", "m", t, r) for t in range(T) for r in range(2)]
    w1 = mm("W1")
    steps += mm("W0")[:T] + [("late",)] + mm("W0")[T:] + w1[:T]
    for t in range(T):
        steps += [w1[T + t], ("gain", t)]
        if t >= 1:
            steps.append(("turn_h", t - 1))
        if t >= 2:
            steps.append(("logits", t - 2))
    steps += [("turn_h", T - 1), ("logits", T - 2), ("logits", T - 1)]
    plan, waiting_hi, waiting_lo = [], [], []
    for s in steps:
        plan.append(s)
        if s[0] in ("mm", "turn", "begin"):
            if waiting_hi:
                plan.append(("hi", *waiting_hi.pop(0)))
            if waiting_lo:
                lo = waiting_lo.pop(0)
                if lo:
                    plan.append(("lo", *lo))
        if s[0] == "mm":
            p = panels[s[1]]
            c = p["ids"][s[2]] + RING
            if s[3] == len(p["outs"]) - 1 and c < len(chunks):
                waiting_hi += [(c, 0), (c, 1)]
                waiting_lo += [None] * (1 + len(waiting_hi) - 2 - len(waiting_lo)) + [(c, 0), (c, 1)]
    assert not waiting_hi and not waiting_lo
    return panels, chunks, units, plan


def build_layer(nc, x, mem, positions, g_mix, w_in, g_mla_q, w_mla_uq, g_mla_kv, w_mla_ukv, w_mla_o,
                swa_sinks, w_swa_o, g_mem, w_mem_kv, w_xa_o, b_gate, w_out, g_ffn, w_router, b_router,
                w_gate_up, b_gate_up, w_down, b_down, g_final, out):
    panels, chunks, units, steps = make_plan()
    weights = dict(w_in=w_in, w_mem_kv=w_mem_kv, w_mla_uq=w_mla_uq, w_mla_ukv=w_mla_ukv,
                   w_mla_o=w_mla_o, w_swa_o=w_swa_o, w_xa_o=w_xa_o, w_out=w_out)
    NF = len(chunks)
    U = len(units)

    owner = []
    ticket_of = {}

    def ticket(key, who):
        ticket_of[key] = len(owner)
        owner.append(who)

    for s in steps:
        if s[0] == "turn":
            ticket(s, "a" if s[1] in BY_SCALAR else "v")
        if s[0] == "mm" and s[2] == 0:
            ticket(("out", s[1], s[3]), "a" if s[1][0] == "G" or s[1] in ("UKV",) else "v")
    for name in ("rank", "count", "GT", "ends"):
        ticket(name, "v")
    for t in range(T):
        for hf in range(2):
            ticket(("bias", t, hf), "v")

    xn_rows = nc.dram_tensor("xn_rows", [SEQ, D], F32, kind="Internal").ap()
    y_rows = nc.dram_tensor("y_rows", [SEQ * TOPK, D], F32, kind="Internal").ap()

    with ExitStack() as ctx:
        base = nc.sbuf_base
        base += (-base) % 64
        K = 1024

        def at(name, shape, dt, kb, extra=0):
            size = int(np.prod(shape[1:])) * (2 if dt == BF16 else 4)
            off = int(kb * K) + extra
            assert base + off + size <= nc.sbuf_top, (name, off, size)
            return nc.alloc_sbuf_tensor_at(name, shape, dt, offset=base + off)

        hi = [at(f"w_hi{i}", [P, 2048], F32R, kb) for i, kb in enumerate((0, 8, 16, 152))]
        lo = [at(f"w_lo{i}", [P, 2048], F32R, kb) for i, kb in enumerate((24, 32, 40, 120))]
        raw = at("w_raw", [P, RING, 2048], F32, 48)
        raw_moe = [at(f"w_raw_moe{i}", [P, 2048], F32, kb) for i, kb in enumerate((48, 56, 64, 188, 72, 80, 88, 160))]
        xT_hi = at("xT_hi", [P, KT, SEQ], F32R, 72)
        xT_lo = at("xT_lo", [P, KT, SEQ], F32R, 88)
        mT_hi = at("mT_hi", [P, KT, SEQ], F32R, 72)
        mT_lo = at("mT_lo", [P, KT, SEQ], F32R, 88)
        rows = at("rows", [P, M + T, D], F32, 104)
        junkf = at("junkf", [P, D], F32, 140)
        junk = at("junk", [P, D], F32, 128)
        ang = at("ang", [P, T, 48], F32, 132)
        ang_k = at("ang_k", [P, T, 48], F32, 133)
        qT = at("qT", [P, MLA_H, SEQ], F32, 104)
        kT = at("kT", [P, MLA_H, SEQ], F32, 120)
        attT_hi = at("attT_hi", [P, 4, SEQ], F32R, 104)
        attT_lo = at("attT_lo", [P, 4, SEQ], F32R, 112)
        merged = at("merged", [P, T, D], F32, 120)
        hs = at("hs", [P, T, D], F32, 104)
        hgT = at("hgT", [P, KT, SEQ], F32, 120)
        memT_hi = at("memT_hi", [P, KT, MEM], F32R, 136)
        memT_lo = at("memT_lo", [P, KT, MEM], F32R, 144)
        qm = at("qm", [P, T, MLA_H, QK], F32, 136)
        km = at("km", [P, T, MLA_H, QK], F32, 148)
        att_mla = at("att_mla", [P, T, 512], F32, 136)
        gate = at("gate", [P, T, 512], F32, 136)
        probs = at("probs", [P, 2, 512], F32, 144)
        probsT = at("probsT", [P, 2, 512], F32, 148)
        rowsB = at("rowsB", [P, T, 512], F32, 152)
        att_xa = at("att_xa", [P, T, 512], F32, 152)
        gmem_b = at("gmem_b", [P, D], F32, 160)
        gmix_b = at("gmix_b", [P, D], F32, 164)
        cT_hi = at("cT_hi", [P, 3, SEQ], F32R, 160)
        cT_lo = at("cT_lo", [P, 3, SEQ], F32R, 166)
        qsT = at("qsT", [P, GRP, SEQ], F32, 160)
        ksT = at("ksT", [P, SEQ], F32, 168)
        vs = at("vs", [P, T, SWA_KV * SD], F32, 170)
        kmr = at("kmr", [P, M, 512], F32, 172)
        vm = at("vm", [P, T, MLA_H * VD], F32, 172)
        att_swa = at("att_swa", [P, T, 512], F32, 172)
        kxT = at("kxT", [P, XA_H, MEM], F32, 180)
        vx = at("vx", [P, M, 512], F32, 184)
        h = at("h", [P, T, D], F32, 172)
        bg_raw = at("bg_raw", [64, 512], F32, 188)
        cqr = at("cqr", [P, T, QR + KVR], F32, 188)
        gq_b = at("gq_b", [P, QR], F32, 194)
        gkv_b = at("gkv_b", [P, KVR], F32, 195)
        krr = at("krr", [P, T, ROPE], F32, 195.5)
        ks_row = at("ks_row", [P, T, SWA_KV * SD], F32, 188)
        qxT = at("qxT", [P, XA_H, SEQ], F32, 188)
        bb_raw = at("bb_raw", [64, 2 * DE], F32, 188)
        ident = at("ident", [P, P], F32, 196)
        ident_h = at("ident_h", [P, P], BF16, 196.5)
        mask_cur = at("mask_cur", [P, P], BF16, 196.75)
        mask_prev = at("mask_prev", [P, P], BF16, 197)
        zero_h = at("zero_h", [P, P], BF16, 197.25)
        below = at("below", [P, P], BF16, 197.5)
        ones = at("ones", [P, P], BF16, 198)
        cosv = at("cosv", [P, T, 48], F32, 198.5)
        sinv = at("sinv", [P, T, 48], F32, 199.25)
        sel = at("sel", [64, P], F32R, 200)
        bg = at("bg", [64, 512], F32R, 200.5)
        ropeA = at("ropeA", [P, 512], F32, 202.5)
        ropeB = at("ropeB", [P, 512], F32, 204.5)
        o = int(206.5 * K)
        small = {}
        for name, n in (("nmax", U), ("mx", 8), ("rsum", U), ("esink", 8), ("stat", 32)):
            small[name] = at(name, [P, n], F32, 0, o)
            o += 4 * n
        nmax, mx, rsum, esink, stat = (small[n] for n in ("nmax", "mx", "rsum", "esink", "stat"))
        sink_b = at("sink_b", [P, 8], F32, 0, o)
        nsink_b = at("nsink_b", [P, 8], F32, 0, o + 32)
        rowid = at("rowid", [64, 1], F32, 0, o + 64)
        rowid_i = at("rowid_i", [64, 1], I32, 0, o + 96)
        pos_i = at("pos_i", [P, T], I32, 0, o + 128)
        posf = at("posf", [P, T], F32, 0, o + 160)
        rowid_f = at("rowid_f", [64, 1], F32, 0, o + 224)
        over_n = at("over_n", [1, 1], I32, 0, o + 192)
        inv_f = at("inv_f", [P, 48], F32, 135)
        exT_hi = at("exT_hi", [P, 2, KT, P], F32R, 96)
        exT_lo = at("exT_lo", [P, 2, KT, P], F32R, 104)
        hT_hi = at("hT_hi", [P, KT, P], F32R, 112)
        hT_lo = at("hT_lo", [P, KT, P], F32R, 116)
        g_sb = at("g_sb", [P, HALF], F32, 128)
        u_sb = at("u_sb", [P, HALF], F32, 130)
        s_sb = at("s_sb", [P, HALF], F32, 132)
        h_sb = at("h_sb", [P, HALF], F32, 134)
        xg = at("xg", [P, D], F32, 136)
        y_sb = at("y_sb", [P, D], F32, 140)
        bb = at("bb", [64, 2 * DE], F32R, 144)
        bdn_raw = at("bdn_raw", [3 * NE, D], F32, 152)
        bdn = at("bdn", [3 * NE, D], F32R, 156)
        gfin_b = at("gfin_b", [P, D], F32, 36)
        gffn_b = at("gffn_b", [P, D], F32, 160)
        onehot = at("onehot", [P, T, TOPK, NE], F32, 128)
        tmp512 = at("tmp512", [P, T, TOPK, NE], F32, 130)
        picks = at("picks", [P, T, P], F32, 168)
        wr = at("wr", [P, KT, NE], F32, 170)
        lg = at("lg", [P, T, NE], F32, 171)
        br_b = at("br_b", [P, NE], F32, 171.5)
        ecol = at("ecol", [64, NE + MAX_OVER], F32, 171.625)
        slots_f = at("slots_f", [P, P], F32, 198.5)
        rank_e = at("rank_e", [P, T, NE], F32, 199)
        val_e = at("val_e", [P, T, NE], F32, 199.5)
        msk = at("msk", [P, T, NE], BF16, 200.5)
        gdense = at("gdense", [P, T, 3, NE], F32, 140)
        over_b = at("over_b", [P, MAX_OVER], F32, 201.5)
        mval = at("mval", [P, T, 8], F32, 201.625)
        midx = at("midx", [P, T, 8], U32, 201.75)
        idxf = at("idxf", [P, T, TOPK], F32, 201.875)
        gk = at("gk", [P, T, TOPK], F32, 201.9375)
        less = at("less", [P, T, TOPK, TOPK], F32, 170)
        at_place = at("at_place", [P, T, TOPK, TOPK], F32, 170.25)
        place_f = at("place_f", [P, T, TOPK], F32, 170.5)
        gates = at("gates", [P, T, TOPK], F32, 202.25)
        asg_i = at("asg_i", [P, T, TOPK], I32, 202)
        asg_f = at("asg_f", [P, T, TOPK], F32, 202.0625)
        lanes_e = at("lanes_e", [P, NE], F32, 202.125)
        lanes_i = at("lanes_i", [P, P], I32, 202.5)
        over_i = at("over_i", [P, MAX_OVER, NE], F32, 204.5)
        upto32 = at("upto32", [NE, NE], F32, 203)
        over = at("over", [NE, P], F32, 203.125)
        ends = at("ends", [P, NE], F32, 203.625)
        over_e = at("over_e", [P, MAX_OVER], F32, 203.75)
        over_ei = at("over_ei", [P, MAX_OVER], I32, 203.8125)
        rank_o = at("rank_o", [P, T], F32, 203.875)
        asg_sb = at("asg_sb", [P, 2], U32, 203.9375)
        tok_sb = at("tok_sb", [P, 2], U32, 204)
        idx_t = at("idx_t", [P, 2], F32, 204.0625)
        rank_c = at("rank_c", [P, T], F32, 204.125)
        GT = at("GT", [3 * NE, SEQ], F32R, 132)
        yk_early = [at(f"yk_early{i}", [P, 2, D], F32, kb) for i, kb in enumerate((48, 56, 64, 188, 72, 80))]
        yk_last = at("yk_last", [P, T, D], F32, 0)
        fin = at("fin", [P, T, D], F32, 16)
        junk2 = at("junk2", [P, D], F32, 32)

        PA = [ctx.enter_context(nc.psum_tensor(f"PA{i}", [P, 512], F32)) for i in range(4)]
        SC = [ctx.enter_context(nc.psum_tensor(f"SC{i}", [P, 512], F32)) for i in range(2)]
        PTb = ctx.enter_context(nc.psum_tensor("PTb", [P, 512], F32))
        OB = ctx.enter_context(nc.psum_tensor("OB", [P, 512], F32))

        def sem(name):
            return ctx.enter_context(nc.semaphore(name))

        consts = sem("consts")
        rows_in = [sem(f"rows_in{i}") for i in range(M + T)]
        gmem_in, gmix_in, pos_in, bg_in = (sem(n) for n in ("gmem_in", "gmix_in", "pos_in", "bg_in"))
        gq_in, gkv_in = sem("gq_in"), sem("gkv_in")
        raw_in = [sem(f"raw_in{i}") for i in range(RING)]
        moe_in = [sem(f"moe_in{i}") for i in range(RAW)]
        hi_ready, lo_ready, used = sem("hi_ready"), sem("lo_ready"), sem("used")
        ticket_done = sem("ticket_done")
        free_v, free_a = sem("free_v"), sem("free_a")
        part_hi = sem("part_hi")
        sq_done, var_done, root_done = sem("sq_done"), sem("var_done"), sem("root_done")
        normed = sem("normed")
        sel_ready, bg_hi, bg_ready = sem("sel_ready"), sem("bg_hi"), sem("bg_ready")
        trig, trig_ready = sem("trig"), sem("trig_ready")
        row_ready = sem("row_ready")
        row_k = sem("row_k")
        s_done, nm_done, exp_done, es_done = sem("s_done"), sem("nm_done"), sem("exp_done"), sem("es_done")
        t_done, pt_done, av_done, o_done = sem("t_done"), sem("pt_done"), sem("av_done"), sem("o_done")
        h_in, late_in, gfin_in = sem("h_in"), sem("late_in"), sem("gfin_in")
        dve_chain = sem("dve_chain")
        hg_ready, h_turned, hT_copied_a, hT_copied_v = (sem(n) for n in ("hg_ready", "h_turned", "hT_copied_a", "hT_copied_v"))
        logits_done, rms_ready = sem("logits_done"), sem("rms_ready")
        hs_ready, hs_stored = sem("hs_ready"), sem("hs_stored")
        mask_ready, over_ready, gd_ready = sem("mask_ready"), sem("over_ready"), sem("gd_ready")
        sub_done, gexp_done = sem("sub_done"), sem("gexp_done")
        biases_hi, biases_ready = sem("biases_hi"), sem("biases_ready")
        route_ready, list_ready, gt_ready = sem("route_ready"), sem("list_ready"), sem("gt_ready")
        xg_clear = sem("xg_clear")
        pick_ready, pick_summed, tok_ready = sem("pick_ready"), sem("pick_summed"), sem("tok_ready")
        shift_ready, rank_copied = sem("shift_ready"), sem("rank_copied")
        xg_in, xt_turned, xt_hi, xt_ready = sem("xg_in"), sem("xt_turned"), sem("xt_hi"), sem("xt_ready")
        gu_done, g_ready, sig_ready, hid_ready = sem("gu_done"), sem("g_ready"), sem("sig_ready"), sem("hid_ready")
        ht_turned, ht_hi, ht_ready = sem("ht_turned"), sem("ht_hi"), sem("ht_ready")
        y_ready, y_stored = sem("y_ready"), sem("y_stored")
        pool_awake = sem("pool_awake")
        yk_in = [[sem(f"yk_in{t}_{k}") for k in range(TOPK)] for t in range(T)]
        find_chain, glu_chain = sem("find_chain"), sem("glu_chain")
        h_final, fsq, fvar, froot, fin_ready, out_done = (sem(n) for n in ("h_final", "fsq", "fvar", "froot", "fin_ready", "out_done"))

        NCONST = 12
        LATE = 8

        def unit_size(unit):
            kind, _, qt = unit
            if kind == "mla":
                return (qt + 1) * P, QK ** -0.5
            if kind == "swa":
                return (P if qt == 0 else 2 * P), SD ** -0.5
            return MEM, XD ** -0.5

        def freed(n):
            who = owner[n]
            return (free_v if who == "v" else free_a), sum(1 for w in owner[:n + 1] if w == who)

        def final_chunk(c):
            return c == panels[chunks[c][0]]["ids"][-1]

        def used_up(c):
            if final_chunk(c):
                name = chunks[c][0]
                return ticket_done, ticket_of[("out", name, len(panels[name]["outs"]) - 1)] + 1
            return used, sum(1 for d in range(c + 1) if not final_chunk(d))

        def turn_of(cc, after_another, before_another):
            if cc == 0 and after_another:
                return -2
            return cc + 1 if cc >= CH - 2 and before_another else cc

        def expert_slot(i, par):
            def slot(w):
                c = par * CH + w
                return c % RAW, i * (2 * CH // RAW) + (c // RAW + 1)
            return slot

        def further_slot(j):
            def slot(w):
                per_block = 2 if w % RAW < CH - RAW else 1
                return w % RAW, j * per_block + (NE * CH // RAW + w // RAW + 1)
            return slot

        NU = sum(1 for c in range(NF) if not final_chunk(c))

        def take(eng, key):
            n = ticket_of[key]
            if n >= 4:
                eng.wait_ge(*freed(n - 4))
            return PA[n % 4]

        def bank(key):
            return PA[ticket_of[key] % 4]

        def turned(s):
            kind, i, pb = s[1], s[2], bank(s)
            if kind == "kx":
                return kxT[:, 2 * i:2 * i + 2, :], pb[:, :].rearrange("p (h n) -> p h n", h=2)
            if kind in ("qm", "km"):
                return (qT if kind == "qm" else kT)[0:QK, i, :], pb[0:QK, :]
            return {"qs": qsT[:, i, :], "ks": ksT[:, :], "qx": qxT[:, i % XA_H, :]}[kind], pb[:, :]

        def yk(t, k):
            m = k * T + t
            return yk_early[m // 2][:, m % 2, :] if k < TOPK - 1 else yk_last[:, t, :]

        block = ctx.enter_context(nc.Block())

        @block.sync
        def _(sp):
            def rows_load(i):
                src = mem[0, i * P:(i + 1) * P, :] if i < M else x[0, (i - M) * P:(i - M + 1) * P, :]
                sp.dma_start(rows[:, i, :], src).then_inc(rows_in[i], 16)

            def chunk_load(c):
                name, w, col, n, k0, per = chunks[c]
                src = weights[w][0, k0 * P:(k0 + per) * P, col:col + n].rearrange("(k p) n -> p k n", p=P)
                dst = raw[:, c % RING, 0:per * n].rearrange("p (k n) -> p k n", k=per)
                if c >= RING:
                    sp.wait_ge(lo_ready, c - RING + 1)
                sp.dma_start(dst, src).then_inc(raw_in[c % RING], 16)

            rows_load(0)
            rows_load(1)
            sp.dma_start(gmem_b[:, :], g_mem[0:1, :].to_broadcast([P, D])).then_inc(gmem_in, 16)
            chunk_load(0)
            rows_load(M)
            rows_load(M + 1)
            chunk_load(1)
            rows_load(M + 2)
            rows_load(M + 3)
            sp.dma_start(gmix_b[:, :], g_mix[0:1, :].to_broadcast([P, D])).then_inc(gmix_in, 16)
            chunk_load(2)
            sp.dma_start(pos_i[:, :], positions[0].rearrange("(t p) -> p t", p=P), allow_slow_non_contiguous=True).then_inc(pos_in, 16)
            sp.wait_ge(consts, NCONST)
            for part in range(2):
                sp.dma_start(bg_raw[32 * part:32 * part + 6, :],
                             b_gate[0].rearrange("(j n) -> j n", n=512)).then_inc(bg_in, 16)
            sp.dma_start(gq_b[:, :], g_mla_q[0:1, :].to_broadcast([P, QR])).then_inc(gq_in, 16)
            sp.dma_start(gkv_b[:, :], g_mla_kv[0:1, :].to_broadcast([P, KVR])).then_inc(gkv_in, 16)
            for c in range(RING, panels["O21"]["ids"][0] + 1):
                chunk_load(c)
            sp.wait_ge(*used_up(panels["O20"]["ids"][0]))
            sp.dma_start(h[:, :, :], x[0].rearrange("(t p) d -> p t d", p=P)).then_inc(h_in, 16)
            chunk_load(panels["W0"]["ids"][0])
            sp.dma_start(gffn_b[:, :], g_ffn[0:1, :].to_broadcast([P, D])).then_inc(late_in, 16)
            sp.dma_start(wr[:, :, :], w_router[0].rearrange("(k p) e -> p k e", p=P)).then_inc(late_in, 16)
            sp.dma_start(br_b[:, :], b_router[0:1, :].to_broadcast([P, NE])).then_inc(late_in, 16)
            for part in range(2):
                sp.dma_start(bb_raw[32 * part:32 * part + 32, :], b_gate_up[0]).then_inc(late_in, 16)
            for part in range(3):
                sp.dma_start(bdn_raw[32 * part:32 * part + 32, :], b_down[0]).then_inc(late_in, 16)
            for c in range(panels["W0"]["ids"][0] + 1, NF):
                chunk_load(c)
            sp.wait_ge(lo_ready, NF)

            def expert_load(e, cc, slot):
                dst = raw_moe[slot][:, :]
                if cc < 8:
                    hf, k0 = cc // 4, (cc % 4) * 2
                    for k in range(2):
                        src = w_gate_up[0, bass.ds(e, 1), (k0 + k) * P:(k0 + k + 1) * P, :] \
                            .rearrange("o p (s f n) -> (o p) s f n", s=2, f=2)[:, :, hf, :]
                        sp.dma_start(dst[:, k * 1024:(k + 1) * 1024].rearrange("p (s n) -> p s n", s=2),
                                     src).then_inc(moe_in[slot], 16)
                else:
                    k0 = (cc - 8) * 2
                    src = w_down[0, bass.ds(e, 1), k0 * P:(k0 + 2) * P, :].rearrange("o (k p) n -> (o p) k n", p=P)
                    sp.dma_start(dst.rearrange("p (k n) -> p k n", k=2), src).then_inc(moe_in[slot], 32)

            def pair_order(first, last):
                order = [(0, 0)] if first else []
                for par in range(2):
                    ahead = not (last and par)
                    order += [(par, cc) for cc in range(1, CH - 2)]
                    order += [(par + 1, 0)] if ahead else []
                    order += [(par, CH - 2), (par, CH - 1)]
                return order

            for c, (par, cc) in enumerate(pair_order(True, False)):
                if c == 3:
                    sp.wait_ge(biases_ready, 1)
                elif c == 4:
                    sp.wait_ge(*used_up(NF - 1))
                elif c == 7:
                    sp.wait_ge(hs_stored, 16 * T)
                elif c >= RAW:
                    sp.wait_ge(lo_ready, NF + c - RAW + 1)
                expert_load(par, cc, c % RAW)

            def pair(i, last):
                for c, (par, cc) in enumerate(pair_order(False, last), 1):
                    sp.wait_ge(lo_ready, i * (2 * CH) + (NF + c - RAW + 1))
                    expert_load(i * 2 + par, cc, c % RAW)

            with sp.Fori(1, NE // 2 - 1) as i:
                pair(i, False)
            pair(NE // 2 - 1, True)
            sp.wait_ge(list_ready, 1)
            n_over = sp.value_load(over_n[0:1, 0:1], min_val=0, max_val=MAX_OVER)

            def y_load(t, k):
                src = y_rows[t * P * TOPK:(t + 1) * P * TOPK, :].rearrange("(p k) d -> p k d", k=TOPK)
                sp.dma_start(yk(t, k), src[:, k, :]).then_inc(yk_in[t][k], 16)

            with sp.If(n_over < 1):
                sp.wait_ge(y_stored, 16 * NE)
                for m in range((TOPK - 1) * T):
                    sp.wait_ge(lo_ready, NF + NE * CH - RAW + m // 2 + 1)
                    y_load(m % T, m // T)
            with sp.If(n_over > 0):
                with sp.Fori(0, MAX_OVER) as j:
                    with sp.If(j < n_over):
                        e = sp.value_load(over_ei[0:1, bass.ds(j, 1)], min_val=0, max_val=NE - 1)
                        for cc in range(CH):
                            sp.wait_ge(lo_ready, j * CH + (NF + NE * CH + (cc - RAW + 1 if cc >= RAW else 0)))
                            expert_load(e, cc, cc % RAW)
            sp.wait_ge(y_stored, n_over * 16 + 16 * (NE + 1))
            y_load(0, TOPK - 1)
            sp.dma_start(gfin_b[:, :], g_final.rearrange("(a d) -> a d", a=1).to_broadcast([P, D])).then_inc(gfin_in, 16)
            for t in range(1, T):
                y_load(t, TOPK - 1)
            with sp.If(n_over > 0):
                for m in range((TOPK - 1) * T):
                    y_load(m % T, m // T)
            for t in range(T):
                sp.wait_ge(fin_ready, t + 1)
                sp.dma_start(out[0, t * P:(t + 1) * P, :], fin[:, t, :]).then_inc(out_done, 16)
            sp.wait_ge(out_done, 16 * T)

        @block.gpsimd
        def _(pool):
            def done(ins):
                ins.then_inc(consts, 1)

            pool.dma_start(sink_b[:, :], swa_sinks[0:1, :].to_broadcast([P, SWA_H])).then_inc(y_stored, 16)
            pool.sem_inc(y_ready, 2)
            pool.sem_inc(gu_done, 2)
            pool.memset(zero_h[:, :], 0.0).then_inc(consts, 1)
            pool.memset(ident[:, :], 0.0).then_inc(consts, 1)
            pool.memset(below[:, :], 1.0).then_inc(consts, 1)
            pool.memset(bg_raw[:, :], 0.0).then_inc(consts, 1)
            for a, n in ((0, 32), (32, 16)):
                for i in range(n):
                    last = pool.memset(inv_f[:, a + i:a + i + 1], float(np.float32(THETA ** (-i / n))))
            last.then_inc(consts, 1)
            pool.iota(rowid_i[:, :], [[0, 1]], channel_multiplier=1).then_inc(consts, 1)
            pool.memset(ones[:, :], 1.0).then_inc(consts, 1)
            pool.wait_ge(consts, 7)
            done(pool.affine_select(out=ident[:, :], in_=ident[:, :], compare_op=ALU.not_equal, fill=1.0,
                                    base=0, pattern=[[-1, P]], channel_multiplier=1))
            done(pool.affine_select(out=ident_h[:, :], in_=zero_h[:, :], compare_op=ALU.not_equal, fill=1.0,
                                    base=0, pattern=[[-1, P]], channel_multiplier=1))
            done(pool.affine_select(out=mask_cur[:, :], in_=zero_h[:, :], compare_op=ALU.is_ge, fill=NEG,
                                    base=0, pattern=[[-1, P]], channel_multiplier=1))
            done(pool.affine_select(out=mask_prev[:, :], in_=zero_h[:, :], compare_op=ALU.is_gt, fill=NEG,
                                    base=0, pattern=[[1, P]], channel_multiplier=-1))
            done(pool.affine_select(out=below[:, :], in_=below[:, :], compare_op=ALU.is_gt, fill=0.0,
                                    base=0, pattern=[[1, P]], channel_multiplier=-1))

            pool.wait_ge(*freed(ticket_of[("out", "O21", T - 1)]))
            pool.iota(lanes_i[:, :], [[1, P]], channel_multiplier=0).then_inc(route_ready, 1)
            pool.iota(asg_i[:, :, :], [[P * TOPK, T], [0, TOPK]], base=1, channel_multiplier=TOPK).then_inc(route_ready, 1)
            pool.iota(over_i[:, :, :], [[1, MAX_OVER], [0, NE]], channel_multiplier=0,
                      allow_small_or_imprecise_dtypes=True).then_inc(route_ready, 1)
            pool.memset(upto32[:, :], 1.0).then_inc(route_ready, 1)
            pool.memset(xg[:, :], 0.0).then_inc(xg_clear, 1)
            pool.wait_ge(route_ready, 4)
            pool.tensor_copy(slots_f[:, :], lanes_i[:, :]).then_inc(route_ready, 1)
            pool.tensor_copy(lanes_e[:, :], lanes_i[:, 0:NE]).then_inc(route_ready, 1)
            pool.tensor_copy(asg_f[:, :, :], asg_i[:, :, :]).then_inc(route_ready, 1)
            pool.tensor_copy(ecol[:, 0:NE], lanes_i[0:64, 0:NE]).then_inc(route_ready, 1)
            pool.affine_select(out=upto32[:, :], in_=upto32[:, :], compare_op=ALU.is_ge, fill=0.0,
                               base=0, pattern=[[1, NE]], channel_multiplier=-1).then_inc(route_ready, 1)
            pool.wait_ge(route_ready, 9)

            def pick(ranks, n):
                pool.wait_ge(pick_summed, n)
                pool.sem_inc(pool_awake, 1)
                for t in range(T):
                    last = pool.tensor_scalar(picks[:, t, :], slots_f[:, :], ranks[:, t:t + 1], None, ALU.is_equal)
                last.then_inc(pick_ready, 1)

            def pick_expert(e, n):
                pool.wait_ge(pick_summed, n)
                pool.tensor_copy(rank_c[:, :], rank_e[:, :, e].rearrange("p t o -> p (t o)")).then_inc(rank_copied, 1)
                pool.wait_ge(rank_copied, n)
                pool.sem_inc(pool_awake, 1)
                pick(rank_c, n)

            def gather(par, n):
                pool.wait_ge(tok_ready, n + 1)
                pool.wait_ge(xt_turned, n * 2)
                pool.sem_inc(pool_awake, 1)
                pool.indirect_dma_start(xg[:, :], None, xn_rows,
                                        bass.IndirectOffsetOnAxis(ap=tok_sb[:, par:par + 1], axis=0),
                                        bounds_check=SEQ - 1, oob_is_err=False).then_inc(xg_in, 16)

            def scatter(par, n):
                pool.wait_ge(y_ready, n * 2 + 4)
                pool.sem_inc(pool_awake, 1)
                pool.indirect_dma_start(y_rows, bass.IndirectOffsetOnAxis(ap=asg_sb[:, par:par + 1], axis=0),
                                        y_sb[:, :], None,
                                        bounds_check=SEQ * TOPK - 1, oob_is_err=False).then_inc(y_stored, 16)

            pool.wait_ge(mask_ready, 2)
            pool.wait_ge(xg_clear, 1)
            pool.wait_ge(hs_stored, 16 * T)
            gather(0, 0)
            pick_expert(slice(1, 2), 1)

            def body(e, par, ahead):
                if ahead >= 1:
                    gather((par + 1) % 2, e + 1)
                if ahead >= 2:
                    pick_expert(bass.ds(e + 2, 1), e + 2)
                scatter(par, e)

            with pool.Fori(0, NE // 2 - 1) as i:
                for par in range(2):
                    body(i * 2 + par, par, 2)
            body(NE - 2, 0, 1)
            body(NE - 1, 1, 0)

            pool.wait_ge(list_ready, 1)
            n_over = pool.value_load(over_n[0:1, 0:1], min_val=0, max_val=MAX_OVER)
            with pool.If(n_over > 0):
                with pool.Fori(0, MAX_OVER) as j:
                    with pool.If(j < n_over):
                        pool.wait_ge(shift_ready, j + 1)
                        pick(rank_o, j + NE)
                        pool.wait_ge(y_stored, j * 16 + 16 * (NE + 1))
                        gather(0, j + NE)
                        scatter(0, j + NE)

        @block.scalar
        def _(act):
            def split(c, part=None):
                size = chunks[c][5] * chunks[c][3]
                a, b = {None: (0, size), 0: (0, size // 2), 1: (size // 2, size)}[part]
                if part != 1:
                    act.wait_ge(raw_in[c % RING], 16 * (c // RING + 1))
                    if c >= RING:
                        act.wait_ge(*used_up(c - RING))
                ins = act.activation(hi[c % RING][:, a:b], raw[:, c % RING, a:b], ACT.Copy)
                if part != 0:
                    ins.then_inc(hi_ready, 1)

            squares = [0]

            def square(src, col):
                if squares[0]:
                    act.wait_ge(sq_done, squares[0])
                squares[0] += 1
                act.activation(junk[:, 0:src.shape[-1]], src, ACT.Square,
                               accum_out=stat[:, col:col + 1]).then_inc(sq_done, 1)

            def angles():
                act.wait_ge(trig, 1)
                act.activation(sinv[:, :, :], ang[:, :, :], ACT.Sin).then_inc(trig_ready, 1)
                act.wait_ge(trig, 2)
                act.activation(cosv[:, :, :], ang_k[:, :, :], ACT.Sin).then_inc(trig_ready, 1)
                act.wait_ge(bg_in, 32)
                act.activation(bg[:, :], bg_raw[:, :], ACT.Copy).then_inc(bg_hi, 1)

            roots = 0
            for s in steps:
                if s[0] == "split":
                    split(s[1])
                elif s[0] == "hi":
                    split(s[1], s[2])
                elif s[0] == "angles":
                    angles()
                elif s[0] == "square":
                    act.wait_ge(rows_in[s[1]], 16)
                    square(rows[:, s[1], :], s[1])
                elif s[0] == "norm":
                    roots += 1
                    act.wait_ge(var_done, roots)
                    a, b = ((0, M), (M, M + T), (8, 16))[s[1]]
                    act.activation(stat[:, a:b], stat[:, a:b], ACT.Sqrt).then_inc(root_done, 1)
                elif s[0] == "turn":
                    kind, n = s[1], ticket_of[s]
                    pb = bank(s)
                    if kind in ("mem", "x", "c", "att", "m"):
                        act.wait_ge(ticket_done, n + 1)
                        v = pb[:, :].rearrange("p (k n) -> p k n", n=P)
                        sc = 1.0
                        if kind == "mem":
                            dst = memT_hi[:, 4 * s[3]:4 * s[3] + 4, s[2] * P:(s[2] + 1) * P]
                        elif kind == "x":
                            dst = xT_hi[:, 4 * s[3]:4 * s[3] + 4, s[2] * P:(s[2] + 1) * P]
                        elif kind == "c":
                            dst, v = cT_hi[:, :, s[2] * P:(s[2] + 1) * P], v[:, 0:3, :]
                        elif kind == "att":
                            dst = attT_hi[:, :, s[3] * P:(s[3] + 1) * P]
                        else:
                            dst, sc = mT_hi[:, 4 * s[3]:4 * s[3] + 4, s[2] * P:(s[2] + 1) * P], 0.5
                        act.activation(dst, v, ACT.Copy, scale=sc).then_inc(part_hi, 1)
                    elif kind in BY_SCALAR:
                        act.wait_ge(ticket_done, n + 1)
                        act.activation(*turned(s), ACT.Copy).then_inc(free_a, 1)
                elif s[0] == "mm":
                    _, name, ci, oi = s
                    p = panels[name]
                    last = ci == len(p["ids"]) - 1
                    key = ("out", name, oi)
                    if last and name == "P0":
                        act.wait_ge(ticket_done, ticket_of[key] + 1)
                        square(bank(key)[:, CQ:CQ + QR], 8 + oi)
                        square(bank(key)[:, CKV:CKV + KVR], 12 + oi)
                    elif last and name == "UKV":
                        t, half = oi // 2, oi % 2
                        act.wait_ge(ticket_done, ticket_of[key] + 1)
                        v = bank(key)[:, :].rearrange("p (h d) -> p h d", h=4)
                        act.activation(km[:, t, 4 * half:4 * half + 4, 0:NOPE], v[:, :, 0:NOPE], ACT.Copy).then_inc(row_k, 1)
                        act.activation(vm[:, t, 256 * half:256 * half + 256].rearrange("p (h d) -> p h d", h=4),
                                       v[:, :, NOPE:NOPE + VD], ACT.Copy).then_inc(free_a, 1)
                    elif last and name[0] == "G":
                        act.wait_ge(ticket_done, ticket_of[key] + 1)
                        b, hf = int(name[1]), int(name[2])
                        if (b, hf) != (0, 0):
                            prev = f"O{b}{hf - 1}" if hf else f"O{b - 1}1"
                            act.wait_ge(*freed(ticket_of[("out", prev, oi)]))
                        act.activation(gate[:, oi, :], bank(key)[:, :], ACT.Tanh, scale=0.5).then_inc(free_a, 1)
                elif s[0] == "S":
                    u = s[1]
                    kind, hh, _ = units[u]
                    act.wait_ge(nm_done, u + 1)
                    if u >= 2:
                        act.wait_ge(t_done, u - 1)
                    if kind == "swa":
                        if u - 32 >= 8:
                            act.wait_ge(o_done, u - 7)
                        act.activation(esink[:, u % 8:u % 8 + 1], nmax[:, u:u + 1], ACT.Exp,
                                       bias=sink_b[:, hh:hh + 1]).then_inc(es_done, 1)
                    n, scale = unit_size(units[u])
                    act.activation(probs[:, u % 2, 0:n], SC[u % 2][:, 0:n], ACT.Exp, bias=nmax[:, u:u + 1], scale=scale,
                                   accum_out=rsum[:, u:u + 1]).then_inc(exp_done, 1)
                elif s[0] == "late":
                    act.wait_ge(late_in, 16 * LATE)
                    act.activation(bb[:, :], bb_raw[:, :], ACT.Copy)
                    act.activation(bdn[:, :], bdn_raw[:, :], ACT.Copy).then_inc(biases_hi, 1)
                elif s[0] == "gain":
                    t = s[1]
                    act.wait_ge(*freed(ticket_of[("out", "W1", t)]))
                    act.wait_ge(sq_done, squares[0])
                    squares[0] += 1
                    act.activation(junkf[:, :], h[:, t, :], ACT.Square, accum_out=stat[:, 16 + t:17 + t]).then_inc(sq_done, 1)
                elif s[0] == "turn_h":
                    t = s[1]
                    act.wait_ge(h_turned, 2 * t + 1)
                    act.activation(hgT[:, 0:4, t * P:(t + 1) * P],
                                   PTb[:, :].rearrange("p (k n) -> p k n", n=P), ACT.Copy).then_inc(hT_copied_a, 1)
                elif s[0] == "T":
                    u = s[1]
                    n, _ = unit_size(units[u])
                    act.wait_ge(t_done, u + 1)
                    if u >= 2:
                        act.wait_ge(av_done, u - 1)
                    act.activation(probsT[:, u % 2, 0:n], PTb[:, 0:n], ACT.Copy).then_inc(pt_done, 1)

            roots += 1
            act.wait_ge(var_done, roots)
            act.activation(stat[:, 16:20], stat[:, 16:20], ACT.Sqrt).then_inc(root_done, 1)
            act.wait_ge(rms_ready, 1)
            act.wait_ge(h_turned, 2 * T)
            for t in range(T):
                act.activation(hs[:, t, :], hs[:, t, :], ACT.Copy, scale=stat[:, 16 + t:17 + t]).then_inc(hs_ready, 1)
            for t in range(T):
                act.wait_ge(hs_ready, t + 1)
                act.dma_start(xn_rows[t * P:(t + 1) * P, :], hs[:, t, :]).then_inc(hs_stored, 16)
            def esplit(w, n, place):
                slot, (rs, loads) = w % ERING, place(w)
                act.wait_ge(moe_in[rs], loads * 32)
                act.wait_ge(used, n * CH + (NU + w - ERING + 1))
                act.activation(hi[slot][:, :], raw_moe[rs][:, :], ACT.Copy).then_inc(hi_ready, 1)

            act.wait_ge(sub_done, 1)
            act.activation(gk[:, :, :], gk[:, :, :], ACT.Exp).then_inc(gexp_done, 1)
            act.wait_ge(*used_up(NF - 1))
            esplit(0, 0, expert_slot(0, 0))
            esplit(1, 0, expert_slot(0, 0))
            esplit(2, 0, expert_slot(0, 0))

            def sigmoid(half, n):
                act.wait_ge(g_ready, n * 2 + half + 1)
                act.activation(s_sb[:, :], g_sb[:, :], ACT.Sigmoid, scale=ALPHA).then_inc(sig_ready, 1)

            def hidden_hi(half, n):
                act.wait_ge(ht_turned, n * 2 + half + 1)
                act.activation(hT_hi[:, 4 * half:4 * half + 4, :],
                               OB[:, :].rearrange("p (k n) -> p k n", n=P), ACT.Copy).then_inc(ht_hi, 1)

            def x_hi(par, r, n):
                act.wait_ge(xt_turned, n * 2 + r + 1)
                act.activation(exT_hi[:, par, 4 * r:4 * r + 4, :],
                               PTb[:, :].rearrange("p (k n) -> p k n", n=P), ACT.Copy).then_inc(xt_hi, 1)

            def y_copy(n, before_another):
                act.wait_ge(used, n * CH + (NU + turn_of(CH - 1, True, before_another) + 1))
                act.wait_ge(y_stored, n * 16 + 16)
                act.activation(y_sb[:, 0:512], SC[0][:, :], ACT.Copy).then_inc(y_ready, 1)
                act.activation(y_sb[:, 512:1024], SC[1][:, :], ACT.Copy).then_inc(y_ready, 1)

            def body(n, par, ahead, place, place_next=None):
                esplit(5, n, place)
                esplit(6, n, place)
                sigmoid(0, n)
                esplit(7, n, place)
                esplit(8, n, place)
                hidden_hi(0, n)
                esplit(9, n, place)
                if ahead:
                    x_hi(1 - par, 0, n + 1)
                esplit(10, n, place)
                sigmoid(1, n)
                if ahead:
                    x_hi(1 - par, 1, n + 1)
                esplit(11, n, place)
                hidden_hi(1, n)
                if ahead:
                    esplit(12, n, place)
                    esplit(1, n + 1, place_next)
                    esplit(2, n + 1, place_next)
                    esplit(3, n + 1, place_next)
                y_copy(n, ahead)
                if ahead:
                    esplit(4, n + 1, place_next)

            x_hi(0, 0, 0)
            x_hi(0, 1, 0)
            act.wait_ge(ticket_done, len(owner))
            esplit(3, 0, expert_slot(0, 0))
            esplit(4, 0, expert_slot(0, 0))
            with act.Fori(0, NE // 2 - 1) as i:
                for par in range(2):
                    body(i * 2 + par, par, True, expert_slot(i, par), expert_slot(i, par + 1))
            body(NE - 2, 0, True, expert_slot(NE // 2 - 1, 0), expert_slot(NE // 2 - 1, 1))
            body(NE - 1, 1, False, expert_slot(NE // 2 - 1, 1))
            act.wait_ge(list_ready, 1)
            n_over = act.value_load(over_n[0:1, 0:1], min_val=0, max_val=MAX_OVER)
            with act.If(n_over > 0):
                with act.Fori(0, MAX_OVER) as j:
                    with act.If(j < n_over):
                        x_hi(0, 0, j + NE)
                        x_hi(0, 1, j + NE)
                        for w in range(5):
                            esplit(w, j + NE, further_slot(j))
                        body(j + NE, 0, False, further_slot(j))
            for t in range(T):
                act.wait_ge(h_final, t + 1)
                if t:
                    act.wait_ge(fsq, t)
                act.activation(junk2[:, :], h[:, t, :], ACT.Square, accum_out=stat[:, 20 + t:21 + t]).then_inc(fsq, 1)
                act.wait_ge(fvar, t + 1)
                act.activation(stat[:, 24 + t:25 + t], stat[:, 24 + t:25 + t], ACT.Sqrt).then_inc(froot, 1)

        @block.tensor
        def _(pe):
            def product(ps, parts, w_hi, w_lo, first, last):
                pe.matmul(ps, parts[0], w_hi, start=first, stop=False)
                pe.matmul(ps, parts[0], w_lo, start=False, stop=False)
                return pe.matmul(ps, parts[1], w_hi, start=False, stop=last)

            def lhs_of(name, oi, k):
                t = panels[name]["outs"][oi][0]
                cols = slice(t * P, (t + 1) * P)
                if name in ("MK", "MV"):
                    return memT_hi[:, k, cols], memT_lo[:, k, cols]
                if name == "UQ":
                    return cT_hi[:, k, cols], cT_lo[:, k, cols]
                if name == "UKV":
                    return cT_hi[:, 2, cols], cT_lo[:, 2, cols]
                if name[0] == "O":
                    return attT_hi[:, k, cols], attT_lo[:, k, cols]
                if name[0] == "W":
                    return mT_hi[:, k, cols], mT_lo[:, k, cols]
                return xT_hi[:, k, cols], xT_lo[:, k, cols]

            def lhs_ready(name, oi):
                t = panels[name]["outs"][oi][0]
                if name in ("MK", "MV"):
                    key = ("turn", "mem", t, 1)
                elif name in ("UQ", "UKV"):
                    key = ("turn", "c", t)
                elif name[0] == "O":
                    key = ("turn", "att", int(name[1]), t)
                elif name[0] == "W":
                    key = ("turn", "m", t, 1)
                else:
                    key = ("turn", "x", t, 1)
                pe.wait_ge(*freed(ticket_of[key]))

            def turn(s):
                kind = s[1]
                ps = take(pe, s)
                if kind in ("mem", "x"):
                    i = s[2] + (M if kind == "x" else 0)
                    pe.wait_ge(normed, i + 1)
                    for j in range(4):
                        k = 4 * s[3] + j
                        last = pe.transpose(ps[:, j * P:(j + 1) * P], rows[:, i, k * P:(k + 1) * P], ident[:, :])
                elif kind == "c":
                    pe.wait_ge(normed, M + T + s[2] + 1)
                    for j in range(3):
                        last = pe.transpose(ps[:, j * P:(j + 1) * P], cqr[:, s[2], j * P:(j + 1) * P], ident[:, :])
                elif kind == "kx":
                    pe.wait_ge(*freed(ticket_of[("out", "MK", 1)]))
                    for j in range(2):
                        for m in range(M):
                            hh = 2 * s[2] + j
                            last = pe.transpose(ps[:, (2 * j + m) * P:(2 * j + m + 1) * P],
                                                kmr[:, m, hh * P:(hh + 1) * P], ident[:, :])
                elif kind in ("qm", "km"):
                    pe.wait_ge(row_ready, 1 + 8)
                    if kind == "km":
                        pe.wait_ge(row_k, 8)
                    for t in range(T):
                        last = pe.transpose(ps[0:QK, t * P:(t + 1) * P], (qm if kind == "qm" else km)[:, t, s[2], :],
                                            ident[:, :])
                elif kind == "qs":
                    pe.wait_ge(row_ready, 9 + 4)
                    for t in range(T):
                        last = pe.transpose(ps[:, t * P:(t + 1) * P], rowsB[:, t, s[2] * P:(s[2] + 1) * P], ident[:, :])
                elif kind == "ks":
                    pe.wait_ge(row_ready, 9 + 8)
                    for t in range(T):
                        last = pe.transpose(ps[:, t * P:(t + 1) * P], ks_row[:, t, :], ident[:, :])
                elif kind == "qx":
                    pe.wait_ge(*freed(ticket_of[("out", "P3", T - 1)]))
                    for t in range(T):
                        last = pe.transpose(ps[:, t * P:(t + 1) * P], rowsB[:, t, s[2] * P:(s[2] + 1) * P], ident[:, :])
                elif kind == "att":
                    src = (att_mla, att_swa, att_xa)[s[2]]
                    pe.wait_ge(o_done, (32, 64, 80)[s[2]])
                    for j in range(4):
                        last = pe.transpose(ps[:, j * P:(j + 1) * P], src[:, s[3], j * P:(j + 1) * P], ident[:, :])
                elif kind == "m":
                    pe.wait_ge(*freed(ticket_of[("out", "O21", T - 1)]))
                    for j in range(4):
                        k = 4 * s[3] + j
                        last = pe.transpose(ps[:, j * P:(j + 1) * P], merged[:, s[2], k * P:(k + 1) * P], ident[:, :])
                last.then_inc(ticket_done, 1)

            def multiply(s):
                kind, name, ci, oi = s
                p = panels[name]
                _, col, n = p["outs"][oi]
                c, per = p["ids"][ci], p["per"]
                key = ("out", name, oi)
                first, final = ci == 0, ci == len(p["ids"]) - 1
                begun = kind == "mm" and ("begin", *s[1:]) in steps
                ps = (take(pe, key) if first and not begun else bank(key))[:, 0:n]
                lhs_ready(name, oi)
                pe.wait_ge(lo_ready, c + 1)
                width = p["n"]
                bias = name[0] == "G"
                for k in (range(per // 2) if kind == "begin" else range(per // 2, per) if begun else range(per)):
                    w = slice(k * width + col, k * width + col + n)
                    last = product(ps, lhs_of(name, oi, ci * per + k), hi[c % RING][:, w], lo[c % RING][:, w],
                                   first and k == 0, final and k == per - 1 and not bias)
                if kind == "begin":
                    return
                if oi == len(p["outs"]) - 1 and not final:
                    last.then_inc(used, 1)
                if final and bias:
                    pe.wait_ge(bg_ready, 1)
                    pe.wait_ge(sel_ready, int(name[1]) * 2 + int(name[2]) + 1)
                    last = pe.matmul(ps, sel[:, :], bg[:, :], start=False, stop=True)
                if final:
                    last.then_inc(ticket_done, 1)

            def scores(u):
                kind, hh, qt = units[u]
                n, _ = unit_size(units[u])
                ps = SC[u % 2]
                if u >= 2:
                    pe.wait_ge(exp_done, u - 1)
                q = slice(qt * P, (qt + 1) * P)
                if kind == "mla":
                    pe.wait_ge(*freed(ticket_of[("turn", "km", hh)]))
                    pe.matmul(ps[:, 0:n], qT[0:QK, hh, q], kT[0:QK, hh, 0:n], start=True, stop=True)
                    last = pe.matmul(ps[:, n - P:n], ident_h[:, :], mask_cur[:, :], start=False, stop=True,
                                     skip_group_check=True)
                elif kind == "swa":
                    g, j = hh // GRP, hh % GRP
                    r = slice(SD * g, SD * (g + 1))
                    pe.wait_ge(*freed(ticket_of[("turn", "ks", 0)]))
                    pe.matmul(ps[:, 0:n], qsT[r, j, q], ksT[r, (qt + 1) * P - n:(qt + 1) * P], start=True, stop=True)
                    if qt:
                        pe.matmul(ps[:, 0:P], ident_h[:, :], mask_prev[:, :], start=False, stop=True,
                                  skip_group_check=True)
                    last = pe.matmul(ps[:, n - P:n], ident_h[:, :], mask_cur[:, :], start=False, stop=True,
                                     skip_group_check=True)
                else:
                    pe.wait_ge(*freed(ticket_of[("turn", "qx", hh)]))
                    last = pe.matmul(ps[:, 0:n], qxT[:, hh, q], kxT[:, hh, :], start=True, stop=True)
                last.then_inc(s_done, 1)

            def turn_probs(u):
                n, _ = unit_size(units[u])
                pe.wait_ge(exp_done, u + 1)
                pe.wait_ge(pt_done, u)
                for j in range(n // P):
                    last = pe.transpose(PTb[:, j * P:(j + 1) * P], probs[:, u % 2, j * P:(j + 1) * P], ident[:, :])
                last.then_inc(t_done, 1)

            def times_v(u):
                kind, hh, qt = units[u]
                n, _ = unit_size(units[u])
                pe.wait_ge(pt_done, u + 1)
                pe.wait_ge(o_done, u)
                blocks = n // P
                for j in range(blocks):
                    kb = j + (qt + 1 - blocks if kind == "swa" else 0)
                    v = {"mla": lambda: vm[:, kb, hh * VD:(hh + 1) * VD],
                         "swa": lambda: vs[:, kb, (hh // GRP) * SD:(hh // GRP + 1) * SD],
                         "xa": lambda: vx[:, kb, hh * XD:(hh + 1) * XD]}[kind]()
                    last = pe.matmul(OB[:, 0:v.shape[-1]], probsT[:, u % 2, j * P:(j + 1) * P], v,
                                     start=(j == 0), stop=(j == blocks - 1))
                last.then_inc(av_done, 1)

            def turn_h(t):
                pe.wait_ge(hg_ready, t + 1)
                for r, ps in enumerate((PTb, OB)):
                    if t == 0:
                        pe.wait_ge(*((pt_done, U), (o_done, U))[r])
                    else:
                        pe.wait_ge((hT_copied_a, hT_copied_v)[r], t)
                    for j in range(4):
                        k = 4 * r + j
                        last = pe.transpose(ps[:, j * P:(j + 1) * P], hs[:, t, k * P:(k + 1) * P], ident[:, :])
                    last.then_inc(h_turned, 1)

            def logits(t):
                if t == 0:
                    pe.wait_ge(exp_done, U)
                    pe.wait_ge(late_in, 16 * LATE)
                pe.wait_ge(hT_copied_a, t + 1)
                pe.wait_ge(hT_copied_v, t + 1)
                for k in range(KT):
                    last = pe.matmul(SC[0][:, t * NE:(t + 1) * NE], hgT[:, k, t * P:(t + 1) * P], wr[:, k, :],
                                     start=(k == 0), stop=(k == KT - 1))
                last.then_inc(logits_done, 1)

            pe.wait_ge(consts, NCONST)
            for s in steps:
                if s[0] == "turn":
                    turn(s)
                elif s[0] in ("begin", "mm"):
                    multiply(s)
                elif s[0] == "S":
                    scores(s[1])
                elif s[0] == "T":
                    turn_probs(s[1])
                elif s[0] == "AV":
                    times_v(s[1])
                elif s[0] == "turn_h":
                    turn_h(s[1])
                elif s[0] == "logits":
                    logits(s[1])

            pe.wait_ge(mask_ready, 1)
            ps = take(pe, "rank")
            for t in range(T):
                for tb in range(t + 1):
                    last = pe.matmul(ps[:, t * NE:(t + 1) * NE], (below if tb == t else ones)[:, :], msk[:, tb, :],
                                     start=(tb == 0), stop=(tb == t))
            last.then_inc(ticket_done, 1)
            ps = take(pe, "count")
            for t in range(T):
                last = pe.matmul(ps[0:NE, 0:P], msk[:, t, :], ones[:, :], start=(t == 0), stop=(t == T - 1))
            last.then_inc(ticket_done, 1)

            def pick_sum(e, n):
                pe.wait_ge(pick_ready, n + 1)
                for t in range(T):
                    last = pe.matmul(PTb[:, 0:1], picks[:, t, :], val_e[:, t, e],
                                     start=(t == 0), stop=(t == T - 1))
                last.then_inc(pick_summed, 1)

            def turn_x(r, n):
                pe.wait_ge(xg_in, n * 16 + 16)
                if r:
                    pe.wait_ge(xt_ready, n * 2 + 1)
                for j in range(4):
                    k = 4 * r + j
                    last = pe.transpose(PTb[:, j * P:(j + 1) * P], xg[:, k * P:(k + 1) * P], ident[:, :])
                last.then_inc(xt_turned, 1)

            def gate_up(cc, n, par, after_another=True):
                w_ = turn_of(cc, after_another, True)
                slot, half = w_ % ERING, cc // 4
                pe.wait_ge(lo_ready, n * CH + (NF + w_ + 1))
                for kk in range(2):
                    k = (cc % 4) * 2 + kk
                    x_h, x_l = exT_hi[:, par, k, :], exT_lo[:, par, k, :]
                    w = [slice(kk * 1024 + s_ * 512, kk * 1024 + (s_ + 1) * 512) for s_ in range(2)]
                    for part, first in ((hi, k == 0), (lo, False)):
                        for s_ in range(2):
                            pe.matmul(PA[2 * half + s_][:, :], x_h, part[slot][:, w[s_]], start=first, stop=False)
                    for s_ in range(2):
                        last = pe.matmul(PA[2 * half + s_][:, :], x_l, hi[slot][:, w[s_]], start=False, stop=False)
                last.then_inc(used, 1)

            def biases(half, n):
                pe.wait_ge(sel_ready, n + 7)
                for s_ in range(2):
                    col = s_ * DE + half * HALF
                    last = pe.matmul(PA[2 * half + s_][:, :], sel[:, :], bb[:, col:col + HALF], start=False, stop=True)
                last.then_inc(gu_done, 1)

            def turn_hidden(half, n):
                pe.wait_ge(hid_ready, n * 2 + half + 1)
                for j in range(4):
                    last = pe.transpose(OB[:, j * P:(j + 1) * P], h_sb[:, j * P:(j + 1) * P], ident[:, :])
                last.then_inc(ht_turned, 1)

            def down(cc, n, before_another):
                w_ = turn_of(cc, True, before_another)
                slot = w_ % ERING
                if cc == 8:
                    pe.wait_ge(ht_ready, n * 2 + 1)
                    pe.wait_ge(y_ready, n * 2 + 2)
                if cc == 10:
                    pe.wait_ge(ht_ready, n * 2 + 2)
                pe.wait_ge(lo_ready, n * CH + (NF + w_ + 1))
                for kk in range(2):
                    k = (cc - 8) * 2 + kk
                    w = [slice(kk * 1024 + s_ * 512, kk * 1024 + (s_ + 1) * 512) for s_ in range(2)]
                    for part, first in ((hi, k == 0), (lo, False)):
                        for s_ in range(2):
                            pe.matmul(SC[s_][:, :], hT_hi[:, k, :], part[slot][:, w[s_]], start=first, stop=False)
                    for s_ in range(2):
                        last = pe.matmul(SC[s_][:, :], hT_lo[:, k, :], hi[slot][:, w[s_]], start=False, stop=(k == KT - 1))
                last.then_inc(used, 1)

            def body(n, par, ahead):
                gate_up(1, n, par)
                if ahead:
                    pick_sum(bass.ds(n + 1, 1), n + 1)
                gate_up(2, n, par)
                gate_up(3, n, par)
                biases(0, n)
                gate_up(4, n, par)
                gate_up(5, n, par)
                turn_hidden(0, n)
                gate_up(6, n, par)
                if ahead:
                    turn_x(0, n + 1)
                gate_up(7, n, par)
                biases(1, n)
                if ahead:
                    turn_x(1, n + 1)
                down(8, n, ahead)
                down(9, n, ahead)
                turn_hidden(1, n)
                if ahead:
                    pe.wait_ge(xt_ready, n * 2 + 4)
                    gate_up(0, n + 1, 1 - par)
                down(10, n, ahead)
                down(11, n, ahead)

            pick_sum(slice(0, 1), 0)
            pe.wait_ge(gd_ready, 1)
            ps = take(pe, "GT")
            for t in range(T):
                last = pe.transpose(ps[0:3 * NE, t * P:(t + 1) * P], gdense[:, t, :, :].rearrange("p a e -> p (a e)"),
                                    ident[:, :])
            last.then_inc(ticket_done, 1)
            pe.wait_ge(over_ready, 1)
            ps = take(pe, "ends")
            pe.matmul(ps[:, 0:NE], over[:, :], upto32[:, :], start=True, stop=True).then_inc(ticket_done, 1)
            pe.wait_ge(gt_ready, 1)
            pe.wait_ge(biases_ready, 1)
            for t in range(T):
                for hf in range(2):
                    ps = take(pe, ("bias", t, hf))
                    pe.matmul(ps[:, :], GT[:, t * P:(t + 1) * P], bdn[:, hf * 512:(hf + 1) * 512],
                              start=True, stop=True).then_inc(ticket_done, 1)
                if t % 2:
                    turn_x(t // 2, 0)
            pe.wait_ge(*freed(len(owner) - 1))
            pe.wait_ge(xt_ready, 2)
            gate_up(0, 0, 0, False)

            with pe.Fori(0, NE // 2 - 1) as i:
                for par in range(2):
                    body(i * 2 + par, par, True)
            body(NE - 2, 0, True)
            body(NE - 1, 1, False)
            pe.wait_ge(list_ready, 1)
            n_over = pe.value_load(over_n[0:1, 0:1], min_val=0, max_val=MAX_OVER)
            with pe.If(n_over > 0):
                with pe.Fori(0, MAX_OVER) as j:
                    with pe.If(j < n_over):
                        e = pe.value_load(over_ei[0:1, bass.ds(j, 1)], min_val=0, max_val=NE - 1)
                        pick_sum(bass.ds(e, 1), j + NE)
                        turn_x(0, j + NE)
                        turn_x(1, j + NE)
                        pe.wait_ge(xt_ready, j * 2 + (NE * 2 + 2))
                        gate_up(0, j + NE, 0, False)
                        body(j + NE, 0, False)

        @block.vector
        def _(dve):
            chain = [0]

            def link(ins):
                chain[0] += 1
                ins.then_inc(dve_chain, 1)
                dve.wait_ge(dve_chain, chain[0])

            def split(c, part=None):
                size = chunks[c][5] * chunks[c][3]
                a, b = {None: (0, size), 0: (0, size // 2), 1: (size // 2, size)}[part]
                dve.wait_ge(hi_ready, c + 1)
                ins = dve.tensor_tensor(lo[c % RING][:, a:b], raw[:, c % RING, a:b],
                                        hi[c % RING][:, a:b].bitcast(F32), ALU.subtract)
                if part != 0:
                    ins.then_inc(lo_ready, 1)

            def rope(src, heads, half, freq, t, dst1, dst2, free, ready):
                s4 = src.rearrange("p h (a d) -> p h a d", a=2)
                n = heads * 2 * half
                A = ropeA[:, 0:n].rearrange("p (h a d) -> p h a d", h=heads, a=2)
                B = ropeB[:, 0:n].rearrange("p (h a d) -> p h a d", h=heads, a=2)
                c = cosv[:, t, freq:freq + half].unsqueeze(1).unsqueeze(1).to_broadcast([P, heads, 2, half])
                s_ = sinv[:, t, freq:freq + half].unsqueeze(1).unsqueeze(1).to_broadcast([P, heads, 2, half])
                link(dve.tensor_tensor(A, s4, c, ALU.mult))
                ins = dve.tensor_tensor(B, s4, s_, ALU.mult)
                link(ins)
                if free:
                    dve.sem_inc(free_v, 1)
                dve.tensor_tensor(dst1, A[:, :, 0, :], B[:, :, 1, :], ALU.subtract).then_inc(dve_chain, 1)
                chain[0] += 1
                last = dve.tensor_tensor(dst2, A[:, :, 1, :], B[:, :, 0, :], ALU.add)
                link(last)
                if ready:
                    dve.sem_inc(row_ready, 1)

            def variance(a, b, width):
                return dve.tensor_scalar(stat[:, a:b], stat[:, a:b], 1.0 / width, EPS, ALU.mult, ALU.add)

            def angles():
                dve.wait_ge(pos_in, 16)
                dve.wait_ge(consts, NCONST)
                link(dve.tensor_copy(rowid_f[:, :], rowid_i[:, :]))
                link(dve.tensor_scalar(rowid[:, :], rowid_f[:, :], 32.0, -32.0, ALU.is_ge, ALU.mult))
                link(dve.tensor_tensor(rowid[:, :], rowid[:, :], rowid_f[:, :], ALU.add))
                link(dve.tensor_copy(posf[:, :], pos_i[:, :]))
                for t in range(T):
                    link(dve.tensor_scalar(ang[:, t, :], inv_f[:, :], posf[:, t:t + 1], None, ALU.mult))
                link(dve.tensor_scalar(ang_k[:, :, :], ang[:, :, :], 1.0 / TWO_PI, ROUND, ALU.mult, ALU.add))
                link(dve.tensor_scalar(ang_k[:, :, :], ang_k[:, :, :], -ROUND, None, ALU.add))
                for part in (PI_A, PI_B, PI_C):
                    link(dve.scalar_tensor_tensor(ang[:, :, :], ang_k[:, :, :], -part, ang[:, :, :], ALU.mult, ALU.add))
                ins = dve.tensor_scalar(ang[:, :, :], ang[:, :, :], PI_SAFE, -PI_SAFE, ALU.min, ALU.max)
                ins.then_inc(trig, 1)
                dve.wait_ge(trig, 1)
                link(dve.scalar_tensor_tensor(ang_k[:, :, :], ang[:, :, :], -1.0, ang[:, :, :], ALU.mult, ALU.min))
                dve.tensor_scalar(ang_k[:, :, :], ang_k[:, :, :], float(np.pi / 2), None, ALU.add).then_inc(trig, 1)
                dve.wait_ge(y_stored, 16)
                link(dve.tensor_scalar(nsink_b[:, :], sink_b[:, :], -1.0, None, ALU.mult))
                dve.wait_ge(bg_hi, 1)
                dve.tensor_tensor(bg[32:64, :], bg_raw[32:64, :], bg[32:64, :].bitcast(F32), ALU.subtract).then_inc(bg_ready, 1)

            n_part, n_sq, roots, n_row = 0, 0, 0, 0
            gates_before = None
            for s in steps:
                if s[0] == "split":
                    split(s[1])
                elif s[0] == "lo":
                    split(s[1], s[2])
                elif s[0] == "angles":
                    angles()
                elif s[0] == "keys":
                    for t in range(T):
                        ins = dve.tensor_copy(km[:, t, :, NOPE:QK], krr[:, t, :].unsqueeze(1)
                                              .to_broadcast([P, MLA_H, ROPE]))
                        if t < T - 1:
                            link(ins)
                    ins.then_inc(row_ready, 1)
                elif s[0] == "norm":
                    roots += 1
                    if s[1] < 2:
                        a, b = ((0, M), (M, M + T))[s[1]]
                        n_sq += b - a
                        dve.wait_ge(sq_done, n_sq)
                        variance(a, b, D).then_inc(var_done, 1)
                        dve.wait_ge(root_done, roots)
                        link(dve.reciprocal(stat[:, a:b], stat[:, a:b]))
                        dve.wait_ge((gmem_in, gmix_in)[s[1]], 16)
                        for i in range(a, b):
                            dve.wait_ge(rows_in[i], 16)
                            dve.scalar_tensor_tensor(rows[:, i, :], rows[:, i, :], stat[:, i:i + 1],
                                                     (gmem_b, gmix_b)[s[1]][:, :], ALU.mult, ALU.mult).then_inc(normed, 1)
                    else:
                        link(variance(8, 12, QR))
                        variance(12, 16, KVR).then_inc(var_done, 1)
                        dve.wait_ge(root_done, roots)
                        link(dve.reciprocal(stat[:, 8:16], stat[:, 8:16]))
                        dve.wait_ge(gq_in, 16)
                        dve.wait_ge(gkv_in, 16)
                        for t in range(T):
                            link(dve.scalar_tensor_tensor(cqr[:, t, 0:QR], cqr[:, t, 0:QR], stat[:, 8 + t:9 + t],
                                                          gq_b[:, :], ALU.mult, ALU.mult))
                            dve.scalar_tensor_tensor(cqr[:, t, QR:], cqr[:, t, QR:], stat[:, 12 + t:13 + t],
                                                     gkv_b[:, :], ALU.mult, ALU.mult).then_inc(normed, 1)
                elif s[0] == "turn":
                    kind, n = s[1], ticket_of[s]
                    pb = bank(s)
                    if kind in ("mem", "x", "c", "att", "m"):
                        n_part += 1
                        dve.wait_ge(part_hi, n_part)
                        v = pb[:, :].rearrange("p (k n) -> p k n", n=P)
                        if kind == "mem":
                            a, b = slice(4 * s[3], 4 * s[3] + 4), slice(s[2] * P, (s[2] + 1) * P)
                            dst, hp = memT_lo[:, a, b], memT_hi[:, a, b]
                        elif kind == "x":
                            a, b = slice(4 * s[3], 4 * s[3] + 4), slice(s[2] * P, (s[2] + 1) * P)
                            dst, hp = xT_lo[:, a, b], xT_hi[:, a, b]
                        elif kind == "c":
                            b = slice(s[2] * P, (s[2] + 1) * P)
                            dst, hp, v = cT_lo[:, :, b], cT_hi[:, :, b], v[:, 0:3, :]
                        elif kind == "att":
                            b = slice(s[3] * P, (s[3] + 1) * P)
                            dst, hp = attT_lo[:, :, b], attT_hi[:, :, b]
                        else:
                            a, b = slice(4 * s[3], 4 * s[3] + 4), slice(s[2] * P, (s[2] + 1) * P)
                            dst, hp = mT_lo[:, a, b], mT_hi[:, a, b]
                        if kind == "m":
                            dve.scalar_tensor_tensor(dst, v, 0.5, hp.bitcast(F32), ALU.mult, ALU.subtract).then_inc(free_v, 1)
                        else:
                            dve.tensor_tensor(dst, v, hp.bitcast(F32), ALU.subtract).then_inc(free_v, 1)
                    elif kind not in BY_SCALAR:
                        dve.wait_ge(ticket_done, n + 1)
                        dve.tensor_copy(*turned(s)).then_inc(free_v, 1)
                elif s[0] == "mm":
                    _, name, ci, oi = s
                    p = panels[name]
                    final = ci == len(p["ids"]) - 1
                    key = ("out", name, oi)
                    ps = bank(key)
                    t = p["outs"][oi][0]
                    if name[0] == "G" and ci == 0 and oi == 0:
                        if gates_before is not None:
                            dve.wait_ge(*freed(ticket_of[("out", gates_before, T - 1)]))
                        gates_before = name
                        dve.tensor_scalar(sel[:, :], rowid[:, 0:1].to_broadcast([64, P]),
                                          float(int(name[1]) * 2 + int(name[2])), None, ALU.is_equal).then_inc(sel_ready, 1)
                    if final and name[0] != "G" and name != "UKV":
                        dve.wait_ge(ticket_done, ticket_of[key] + 1)
                        if name == "MK":
                            dve.tensor_copy(kmr[:, oi, :], ps[:, :]).then_inc(free_v, 1)
                        elif name == "MV":
                            dve.tensor_copy(vx[:, oi, :], ps[:, :]).then_inc(free_v, 1)
                        elif name == "P0":
                            n_sq += 2
                            dve.wait_ge(sq_done, n_sq)
                            dve.wait_ge(bg_ready, 1)
                            link(dve.tensor_copy(cqr[:, t, :], ps[:, CQ:CKR]))
                            dve.wait_ge(trig_ready, 2)
                            rope(ps[:, CKR:CQS].rearrange("p (h d) -> p h d", h=1), 1, ROPE // 2, 32, t,
                                 krr[:, t, 0:ROPE // 2].unsqueeze(1), krr[:, t, ROPE // 2:].unsqueeze(1), True, False)
                        elif name == "UQ":
                            half = oi % 2
                            v = ps[:, 0:384].rearrange("p (h d) -> p h d", h=4)
                            q = qm[:, t, 4 * half:4 * half + 4, :]
                            link(dve.tensor_copy(q[:, :, 0:NOPE], v[:, :, 0:NOPE]))
                            rope(v[:, :, NOPE:QK], 4, ROPE // 2, 32, t, q[:, :, NOPE:NOPE + ROPE // 2],
                                 q[:, :, NOPE + ROPE // 2:QK], True, True)
                        elif name == "P1":
                            q = rowsB[:, t, :].rearrange("p (j g a d) -> p g j a d", j=GRP, g=SWA_KV, a=2)
                            v = ps[:, :].rearrange("p (g j d) -> p g j d", g=SWA_KV, j=GRP)
                            for g in range(SWA_KV):
                                rope(v[:, g], GRP, SD // 2, 0, t, q[:, g, :, 0, :], q[:, g, :, 1, :],
                                     g == SWA_KV - 1, g == SWA_KV - 1)
                        elif name == "P2":
                            link(dve.tensor_copy(vs[:, t, :], ps[:, P:2 * P]))
                            v = ps[:, 0:P].rearrange("p (g d) -> p g d", g=SWA_KV)
                            q = ks_row[:, t, :].rearrange("p (g a d) -> p g a d", g=SWA_KV, a=2)
                            rope(v, SWA_KV, SD // 2, 0, t, q[:, :, 0, :], q[:, :, 1, :], True, True)
                        elif name == "P3":
                            dve.tensor_copy(rowsB[:, t, :], ps[:, :]).then_inc(free_v, 1)
                        elif name[0] == "O":
                            b, hf = int(name[1]), int(name[2])
                            dve.wait_ge(*freed(ticket_of[("out", f"G{b}{hf}", t)]))
                            m = merged[:, t, hf * 512:(hf + 1) * 512]
                            if b == 0:
                                dve.scalar_tensor_tensor(m, gate[:, t, :], 1.0, ps[:, :], ALU.add, ALU.mult).then_inc(free_v, 1)
                            else:
                                gated = (ropeA, ropeB)[t % 2]
                                link(dve.scalar_tensor_tensor(gated[:, :], gate[:, t, :], 1.0, ps[:, :], ALU.add, ALU.mult))
                                dve.tensor_tensor(m, m, gated[:, :], ALU.add).then_inc(free_v, 1)
                        elif name[0] == "W":
                            hf = int(name[1])
                            dve.wait_ge(h_in, 16)
                            m = h[:, t, hf * 512:(hf + 1) * 512]
                            dve.tensor_tensor(m, m, ps[:, :], ALU.add).then_inc(free_v, 1)
                elif s[0] == "S":
                    u = s[1]
                    kind, hh, _ = units[u]
                    n, scale = unit_size(units[u])
                    dve.wait_ge(s_done, u + 1)
                    link(dve.reduce_max(mx[:, u % 8:u % 8 + 1], SC[u % 2][:, 0:n], AX.X))
                    if kind == "swa":
                        dve.tensor_scalar(nmax[:, u:u + 1], mx[:, u % 8:u % 8 + 1], -scale, nsink_b[:, hh:hh + 1],
                                          ALU.mult, ALU.min).then_inc(nm_done, 1)
                    else:
                        dve.tensor_scalar(nmax[:, u:u + 1], mx[:, u % 8:u % 8 + 1], -scale, None,
                                          ALU.mult).then_inc(nm_done, 1)
                elif s[0] == "late":
                    dve.wait_ge(biases_hi, 1)
                    dve.tensor_tensor(bb[32:64, :], bb_raw[32:64, :], bb[32:64, :].bitcast(F32), ALU.subtract)
                    dve.tensor_tensor(bdn[64:96, :], bdn_raw[64:96, :], bdn[64:96, :].bitcast(F32),
                                      ALU.subtract).then_inc(biases_ready, 1)
                elif s[0] == "gain":
                    t = s[1]
                    dve.wait_ge(*freed(ticket_of[("out", "W1", t)]))
                    dve.wait_ge(late_in, 16 * LATE)
                    dve.tensor_tensor(hs[:, t, :], h[:, t, :], gffn_b[:, :], ALU.mult).then_inc(hg_ready, 1)
                elif s[0] == "turn_h":
                    t = s[1]
                    dve.wait_ge(h_turned, 2 * t + 2)
                    dve.tensor_copy(hgT[:, 4:8, t * P:(t + 1) * P],
                                    OB[:, :].rearrange("p (k n) -> p k n", n=P)).then_inc(hT_copied_v, 1)
                elif s[0] == "AV":
                    u = s[1]
                    kind, hh, qt = units[u]
                    width = XD if kind == "xa" else VD
                    dst = {"mla": att_mla, "swa": att_swa, "xa": att_xa}[kind][:, qt, hh * width:(hh + 1) * width]
                    dve.wait_ge(exp_done, u + 1)
                    r = rsum[:, u:u + 1]
                    if kind == "swa":
                        dve.wait_ge(es_done, u - 31)
                        link(dve.tensor_tensor(r, r, esink[:, u % 8:u % 8 + 1], ALU.add))
                    link(dve.reciprocal(r, r))
                    dve.wait_ge(av_done, u + 1)
                    dve.tensor_scalar(dst, OB[:, 0:width], r, None, ALU.mult).then_inc(o_done, 1)

            dve.wait_ge(sq_done, n_sq + T)
            roots += 1
            variance(16, 20, D).then_inc(var_done, 1)
            dve.wait_ge(root_done, roots)
            link(dve.reciprocal(stat[:, 16:20], stat[:, 16:20]))
            dve.sem_inc(rms_ready, 1)
            dve.wait_ge(logits_done, T)
            for t in range(T):
                link(dve.scalar_tensor_tensor(lg[:, t, :], SC[0][:, t * NE:(t + 1) * NE], stat[:, 16 + t:17 + t],
                                              br_b[:, :], ALU.mult, ALU.add))
            for t in range(T):
                link(dve.max(mval[:, t, :], lg[:, t, :]))
            for t in range(T):
                link(dve.max_index(midx[:, t, :], mval[:, t, :], lg[:, t, :]))
            dve.tensor_tensor(gk[:, :, :], mval[:, :, 0:TOPK], mval[:, :, 0:1].to_broadcast([P, T, TOPK]),
                              ALU.subtract).then_inc(sub_done, 1)
            link(dve.tensor_copy(idxf[:, :, :], midx[:, :, 0:TOPK]))
            dve.wait_ge(route_ready, 9)

            def over_experts(x):
                return x[:, :, :].unsqueeze(3).to_broadcast([P, T, TOPK, NE])

            def by_expert(x):
                return x[:, :, :, :].rearrange("p t k e -> p t e k")

            link(dve.tensor_tensor(onehot[:, :, :, :], over_experts(idxf),
                                   lanes_e[:, :].unsqueeze(1).unsqueeze(1).to_broadcast([P, T, TOPK, NE]), ALU.is_equal))
            dve.tensor_reduce(msk[:, :, :], by_expert(onehot), AX.X, ALU.max).then_inc(mask_ready, 1)
            link(dve.tensor_tensor(less[:, :, :, :], idxf[:, :, :].unsqueeze(2).to_broadcast([P, T, TOPK, TOPK]),
                                   idxf[:, :, :].unsqueeze(3).to_broadcast([P, T, TOPK, TOPK]), ALU.is_lt))
            link(dve.tensor_reduce(place_f[:, :, :], less[:, :, :, :], AX.X, ALU.add))
            link(dve.tensor_tensor(asg_f[:, :, :], asg_f[:, :, :], place_f[:, :, :], ALU.add))
            link(dve.tensor_tensor(tmp512[:, :, :, :], onehot[:, :, :, :], over_experts(asg_f), ALU.mult))
            link(dve.tensor_reduce(val_e[:, :, :], by_expert(tmp512), AX.X, ALU.add))
            dve.wait_ge(ticket_done, ticket_of["rank"] + 1)
            dve.wait_ge(mask_ready, 1)
            ins = dve.scalar_tensor_tensor(rank_e[:, :, :], bank("rank")[:, 0:T * NE].rearrange("p (t e) -> p t e", t=T),
                                           1.0, msk[:, :, :], ALU.add, ALU.mult)
            ins.then_inc(free_v, 1)
            dve.wait_ge(*freed(ticket_of["rank"]))
            dve.tensor_scalar(rank_e[:, :, :], rank_e[:, :, :], -1.0, None, ALU.add).then_inc(mask_ready, 1)
            dve.wait_ge(mask_ready, 2)
            for t in range(T):
                last = dve.tensor_scalar(picks[:, t, :], slots_f[:, :], rank_e[:, t, 0:1], None, ALU.is_equal)
            last.then_inc(pick_ready, 1)

            def find_rows(par, n, blocks_stored):
                dve.wait_ge(pick_summed, n + 1)
                dve.wait_ge(y_stored, blocks_stored * 16 + 16)
                p1 = PTb[:, 0:1]
                dve.tensor_scalar(idx_t[:, 0:1], p1, 0.0, NOWHERE, ALU.is_equal, ALU.mult).then_inc(find_chain, 1)
                dve.wait_ge(find_chain, n * 3 - 2)
                dve.scalar_tensor_tensor(idx_t[:, 1:2], p1, -1.0, idx_t[:, 0:1], ALU.add, ALU.add).then_inc(find_chain, 1)
                dve.wait_ge(find_chain, n * 3 - 1)
                dve.tensor_copy(asg_sb[:, par:par + 1], idx_t[:, 1:2]).then_inc(find_chain, 1)
                dve.wait_ge(find_chain, n * 3)
                dve.tensor_scalar(tok_sb[:, par:par + 1], asg_sb[:, par:par + 1], 2, None,
                                  ALU.logical_shift_right).then_inc(tok_ready, 1)

            def esplit(w, n, place):
                slot, rs = w % ERING, place(w)[0]
                dve.wait_ge(hi_ready, n * CH + (NF + w + 1))
                dve.tensor_tensor(lo[slot][:, :], raw_moe[rs][:, :], hi[slot][:, :].bitcast(F32),
                                  ALU.subtract).then_inc(lo_ready, 1)

            esplit(0, 0, expert_slot(0, 0))
            dve.wait_ge(pick_summed, 1)
            link(dve.tensor_scalar(idx_t[:, 0:1], PTb[:, 0:1], 0.0, NOWHERE, ALU.is_equal, ALU.mult))
            link(dve.scalar_tensor_tensor(idx_t[:, 1:2], PTb[:, 0:1], -1.0, idx_t[:, 0:1], ALU.add, ALU.add))
            link(dve.tensor_copy(asg_sb[:, 0:1], idx_t[:, 1:2]))
            dve.tensor_scalar(tok_sb[:, 0:1], asg_sb[:, 0:1], 2, None, ALU.logical_shift_right).then_inc(tok_ready, 1)
            dve.wait_ge(gexp_done, 1)
            gsum = mx[:, 0:T]
            link(dve.reduce_sum(gsum, gk[:, :, :], AX.X))
            link(dve.reciprocal(gsum, gsum))
            link(dve.tensor_tensor(gk[:, :, :], gk[:, :, :], gsum.unsqueeze(2).to_broadcast([P, T, TOPK]), ALU.mult))
            link(dve.tensor_tensor(at_place[:, :, :, :], place_f[:, :, :].unsqueeze(2).to_broadcast([P, T, TOPK, TOPK]),
                                   slots_f[:, 0:TOPK].unsqueeze(1).unsqueeze(3).to_broadcast([P, T, TOPK, TOPK]),
                                   ALU.is_equal))
            link(dve.tensor_tensor(at_place[:, :, :, :], at_place[:, :, :, :],
                                   gk[:, :, :].unsqueeze(2).to_broadcast([P, T, TOPK, TOPK]), ALU.mult))
            link(dve.tensor_reduce(gates[:, :, :], at_place[:, :, :, :], AX.X, ALU.add))
            link(dve.tensor_tensor(tmp512[:, :, :, :], onehot[:, :, :, :], over_experts(gk), ALU.mult))
            link(dve.tensor_reduce(gdense[:, :, 0, :], by_expert(tmp512), AX.X, ALU.add))
            dve.tensor_copy(gdense[:, :, 1:3, :], gdense[:, :, 0:1, :].to_broadcast([P, T, 2, NE])).then_inc(gd_ready, 1)
            dve.wait_ge(ticket_done, ticket_of["count"] + 1)
            cnt = bank("count")[0:NE, 0:P]
            link(dve.tensor_scalar(over[:, :], cnt, float(P), None, ALU.is_gt))
            link(dve.scalar_tensor_tensor(over[:, :], cnt, float(2 * P), over[:, :], ALU.is_gt, ALU.add))
            ins = dve.scalar_tensor_tensor(over[:, :], cnt, float(3 * P), over[:, :], ALU.is_gt, ALU.add)
            link(ins)
            dve.sem_inc(free_v, 1)
            dve.sem_inc(over_ready, 1)
            dve.wait_ge(ticket_done, ticket_of["GT"] + 1)
            link(dve.tensor_copy(GT[:, :], bank("GT")[0:3 * NE, :]))
            link(dve.tensor_tensor(GT[NE:2 * NE, :], bank("GT")[NE:2 * NE, :], GT[NE:2 * NE, :].bitcast(F32), ALU.subtract))
            dve.sem_inc(free_v, 1)
            dve.sem_inc(gt_ready, 1)
            dve.wait_ge(ticket_done, ticket_of["ends"] + 1)
            link(dve.tensor_copy(ends[:, :], bank("ends")[:, 0:NE]))
            dve.sem_inc(free_v, 1)

            esplit(1, 0, expert_slot(0, 0))

            def x_lo(par, r, n):
                dve.wait_ge(xt_hi, n * 2 + r + 1)
                a = slice(4 * r, 4 * r + 4)
                dve.tensor_tensor(exT_lo[:, par, a, :], PTb[:, :].rearrange("p (k n) -> p k n", n=P),
                                  exT_hi[:, par, a, :].bitcast(F32), ALU.subtract).then_inc(xt_ready, 1)

            def swiglu(half, n):
                dve.wait_ge(gu_done, n * 2 + half + 3)
                dve.tensor_scalar(g_sb[:, :], PA[2 * half][:, :], LIMIT, None, ALU.min).then_inc(g_ready, 1)
                dve.tensor_scalar(u_sb[:, :], PA[2 * half + 1][:, :], LIMIT, -LIMIT, ALU.min, ALU.max).then_inc(glu_chain, 1)
                dve.wait_ge(glu_chain, n * 4 + (2 * half + 1))
                dve.wait_ge(g_ready, n * 2 + half + 1)
                dve.scalar_tensor_tensor(u_sb[:, :], u_sb[:, :], 1.0, g_sb[:, :],
                                         ALU.add, ALU.mult).then_inc(glu_chain, 1)
                dve.wait_ge(glu_chain, n * 4 + (2 * half + 2))
                dve.wait_ge(sig_ready, n * 2 + half + 1)
                dve.tensor_tensor(h_sb[:, :], u_sb[:, :], s_sb[:, :], ALU.mult).then_inc(hid_ready, 1)

            def hidden_lo(half, n):
                dve.wait_ge(ht_hi, n * 2 + half + 1)
                a = slice(4 * half, 4 * half + 4)
                dve.tensor_tensor(hT_lo[:, a, :], OB[:, :].rearrange("p (k n) -> p k n", n=P),
                                  hT_hi[:, a, :].bitcast(F32), ALU.subtract).then_inc(ht_ready, 1)

            def select(n):
                dve.wait_ge(gu_done, n * 2 + 2)
                dve.tensor_scalar(sel[:, :], ecol[:, bass.ds(n, 1)].to_broadcast([64, P]), rowid[:, 0:1], None,
                                  ALU.is_equal).then_inc(sel_ready, 1)

            def body(n, par, ahead, place, place_next=None):
                select(n)
                if ahead:
                    find_rows(1 - par, n + 1, n)
                esplit(5, n, place)
                esplit(6, n, place)
                swiglu(0, n)
                esplit(7, n, place)
                esplit(8, n, place)
                hidden_lo(0, n)
                esplit(9, n, place)
                if ahead:
                    x_lo(1 - par, 0, n + 1)
                esplit(10, n, place)
                swiglu(1, n)
                if ahead:
                    x_lo(1 - par, 1, n + 1)
                esplit(11, n, place)
                hidden_lo(1, n)
                if ahead:
                    esplit(12, n, place)
                    esplit(1, n + 1, place_next)
                    esplit(2, n + 1, place_next)
                    esplit(3, n + 1, place_next)
                    esplit(4, n + 1, place_next)

            for t in range(T):
                for hf in range(2):
                    key = ("bias", t, hf)
                    dve.wait_ge(ticket_done, ticket_of[key] + 1)
                    m = h[:, t, hf * 512:(hf + 1) * 512]
                    dve.tensor_tensor(m, m, bank(key)[:, :], ALU.add).then_inc(free_v, 1)
                if t % 2:
                    x_lo(0, t // 2, 0)
            esplit(2, 0, expert_slot(0, 0))
            is_past = tmp512[:, :, :, :].rearrange("p t k e -> p (t k) e")
            past_end = onehot[:, :, :, :].rearrange("p t k e -> p (t k) e")
            ends_b = ends[:, :].unsqueeze(1).to_broadcast([P, MAX_OVER, NE])
            link(dve.tensor_tensor(is_past, ends_b, over_i[:, :, :], ALU.is_le))
            link(dve.tensor_tensor(past_end, is_past, ends_b, ALU.mult))
            link(dve.tensor_reduce(over_e[:, :], is_past, AX.X, ALU.add))
            link(dve.tensor_reduce(over_b[:, :], past_end, AX.X, ALU.max))
            link(dve.tensor_scalar(over_e[:, :], over_e[:, :], float(NE - 1), None, ALU.min))
            link(dve.scalar_tensor_tensor(over_b[:, :], over_b[:, :], -1.0, over_i[:, :, 0], ALU.mult, ALU.add))
            link(dve.tensor_scalar(over_b[:, :], over_b[:, :], 1.0, float(P), ALU.add, ALU.mult))
            link(dve.tensor_copy(over_ei[:, :], over_e[:, :]))
            link(dve.tensor_copy(ecol[:, NE:], over_e[0:64, :]))
            dve.tensor_copy(over_n[:, :], ends[0:1, NE - 1:NE]).then_inc(list_ready, 1)
            esplit(3, 0, expert_slot(0, 0))
            esplit(4, 0, expert_slot(0, 0))
            with dve.Fori(0, NE // 2 - 1) as i:
                for par in range(2):
                    body(i * 2 + par, par, True, expert_slot(i, par), expert_slot(i, par + 1))
            body(NE - 2, 0, True, expert_slot(NE // 2 - 1, 0), expert_slot(NE // 2 - 1, 1))
            body(NE - 1, 1, False, expert_slot(NE // 2 - 1, 1))
            n_over = dve.value_load(over_n[0:1, 0:1], min_val=0, max_val=MAX_OVER)
            with dve.If(n_over > 0):
                with dve.Fori(0, MAX_OVER) as j:
                    with dve.If(j < n_over):
                        e = dve.value_load(over_ei[0:1, bass.ds(j, 1)], min_val=0, max_val=NE - 1)
                        dve.wait_ge(pick_ready, j + NE)
                        dve.tensor_scalar(rank_o[:, :], rank_e[:, :, bass.ds(e, 1)].rearrange("p t o -> p (t o)"),
                                          over_b[:, bass.ds(j, 1)], None, ALU.subtract).then_inc(shift_ready, 1)
                        find_rows(0, j + NE, j + NE)
                        x_lo(0, 0, j + NE)
                        x_lo(0, 1, j + NE)
                        for w in range(5):
                            esplit(w, j + NE, further_slot(j))
                        body(j + NE, 0, False, further_slot(j))

            def finish(t):
                dve.wait_ge(fsq, t + 1)
                if t == 0:
                    dve.wait_ge(gfin_in, 16)
                dve.tensor_scalar(stat[:, 24 + t:25 + t], stat[:, 20 + t:21 + t], 1.0 / D, EPS,
                                  ALU.mult, ALU.add).then_inc(fvar, 1)
                dve.wait_ge(froot, t + 1)
                link(dve.reciprocal(stat[:, 24 + t:25 + t], stat[:, 24 + t:25 + t]))
                dve.scalar_tensor_tensor(fin[:, t, :], h[:, t, :], stat[:, 24 + t:25 + t], gfin_b[:, :],
                                         ALU.mult, ALU.mult).then_inc(fin_ready, 1)

            def weigh(t, k):
                dve.wait_ge(yk_in[t][k], 16)
                return dve.scalar_tensor_tensor(h[:, t, :], yk(t, k), gates[:, t, k:k + 1], h[:, t, :],
                                                ALU.mult, ALU.add)

            for k in range(TOPK - 1):
                for t in range(T):
                    link(weigh(t, k))
            for t in range(T):
                weigh(t, TOPK - 1).then_inc(h_final, 1)
                dve.wait_ge(h_final, t + 1)
                if t:
                    finish(t - 1)
            finish(T - 1)


_INS = ["x", "mem", "positions", "g_mix", "w_in", "g_mla_q", "w_mla_uq", "g_mla_kv", "w_mla_ukv", "w_mla_o",
        "swa_sinks", "w_swa_o", "g_mem", "w_mem_kv", "w_xa_o", "b_gate", "w_out", "g_ffn", "w_router",
        "b_router", "w_gate_up", "b_gate_up", "w_down", "b_down", "g_final"]


def kernel(**inputs):
    import numpy as _np
    import concourse.bacc as _bacc
    from concourse import mybir as _mybir
    from concourse.bass_utils import run_bass_kernel_spmd as _run

    nc = _bacc.Bacc("TRN2", target_bir_lowering=False, num_devices=1)
    arrays, args = {}, []
    for name in _INS:
        a = _np.ascontiguousarray(inputs[name])
        arrays[f"in_{name}"] = a
        args.append(nc.dram_tensor(f"in_{name}", a.shape, _mybir.dt.from_np(a.dtype), kind="ExternalInput").ap())
    out = nc.dram_tensor("out", (1, SEQ, D), F32, kind="ExternalOutput").ap()
    build_layer(nc, *args, out)
    r = _run(nc, [arrays], core_ids=[0])
    return r.results[0]["out"]
```
